# Optimizing a Trainium2 kernel written in Bass

```python
import jax, jax.numpy as jnp
from jax import lax
import numpy as np

D_MODEL = 2048
BATCH = 1
SEQ = 1024
DEPTH = 1

POOL_WINDOWS = (2, 4, 8, 16)
POOL_GROUPS = 4
POOL_GROUP_DIM = D_MODEL // 8
POOL_WIDTH = POOL_GROUPS * POOL_GROUP_DIM
MAX_POOL_WINDOW = 16
HEAD_DIM = 64
N_Q_HEADS = D_MODEL // 128
N_KV_HEADS = 4
Q_PER_KV = N_Q_HEADS // N_KV_HEADS
ATTN_WIDTH = N_Q_HEADS * HEAD_DIM
KV_WIDTH = N_KV_HEADS * HEAD_DIM
WINDOW = 128
BLOCK = 128
N_BRANCHES = 2
DEEPNORM_ALPHA = (2 * DEPTH) ** 0.25
DEEPNORM_BETA = (8 * DEPTH) ** -0.25
LN_EPS = 1e-5
OFF_PGATE = POOL_WIDTH
OFF_Q = 2 * POOL_WIDTH
OFF_K = OFF_Q + ATTN_WIDTH
OFF_V = OFF_K + KV_WIDTH
OFF_AGATE = OFF_V + KV_WIDTH
OFF_MERGE = OFF_AGATE + ATTN_WIDTH
N_IN = OFF_MERGE + N_BRANCHES * D_MODEL

kernel_name = "hybrid_pool_swa_sink_gated_deepnorm"

def _layernorm(x, g, b):
    xf = x.astype(jnp.float32)
    mu = jnp.mean(xf, axis=-1, keepdims=True)
    var = jnp.mean(jnp.square(xf - mu), axis=-1, keepdims=True)
    return ((xf - mu) * lax.rsqrt(var + LN_EPS) * g + b).astype(x.dtype)

def _pool_mixer(p, w_grp, scale):
    B, S, _ = p.shape
    cs = jnp.cumsum(p.astype(jnp.float32), axis=1)
    cs = jnp.pad(cs, ((0, 0), (MAX_POOL_WINDOW, 0), (0, 0)))
    pos = jnp.arange(S)
    pooled = []
    for g, w in enumerate(POOL_WINDOWS):
        lo, hi = g * POOL_GROUP_DIM, (g + 1) * POOL_GROUP_DIM
        win_sum = cs[:, MAX_POOL_WINDOW:, lo:hi] - cs[:, MAX_POOL_WINDOW - w:MAX_POOL_WINDOW - w + S, lo:hi]
        count = jnp.minimum(pos + 1, w).astype(jnp.float32)[None, :, None]
        pooled.append(win_sum / count)
    pooled = jnp.concatenate(pooled, axis=-1).astype(p.dtype) - p
    pooled = pooled.reshape(B, S, POOL_GROUPS, POOL_GROUP_DIM)
    mixed = jnp.einsum('bsgc,gcd->bsgd', pooled, w_grp).reshape(B, S, POOL_WIDTH)
    return mixed * scale

def _sliding_window_attention(q, k, v, sinks):
    B, S, _ = q.shape
    nb = S // BLOCK
    qb = q.reshape(B, nb, BLOCK, N_KV_HEADS, Q_PER_KV, HEAD_DIM)
    kb = k.reshape(B, nb, BLOCK, N_KV_HEADS, HEAD_DIM)
    vb = v.reshape(B, nb, BLOCK, N_KV_HEADS, HEAD_DIM)

    def with_prev(t):
        prev = jnp.pad(t[:, :-1], ((0, 0), (1, 0), (0, 0), (0, 0), (0, 0)))
        return jnp.concatenate([prev, t], axis=2)

    kw, vw = with_prev(kb), with_prev(vb)
    scores = jnp.einsum('bnqhgd,bnkhd->bnhgqk', qb, kw).astype(jnp.float32) * (HEAD_DIM ** -0.5)
    qi = jnp.arange(BLOCK)[:, None]
    kj = jnp.arange(2 * BLOCK)[None, :]
    rel = BLOCK + qi - kj
    band = (rel >= 0) & (rel < WINDOW)
    key_pos = jnp.arange(nb)[:, None] * BLOCK - BLOCK + kj
    valid = band[None] & (key_pos >= 0)[:, None, :]
    scores = jnp.where(valid[None, :, None, None], scores, -jnp.inf)
    sink = sinks.astype(jnp.float32).reshape(N_KV_HEADS, Q_PER_KV)[None, None, :, :, None, None]
    m = jnp.maximum(jnp.max(scores, axis=-1, keepdims=True), sink)
    e = jnp.exp(scores - m)
    probs = (e / (jnp.sum(e, axis=-1, keepdims=True) + jnp.exp(sink - m))).astype(v.dtype)
    o = jnp.einsum('bnhgqk,bnkhd->bnqhgd', probs, vw)
    return o.reshape(B, S, ATTN_WIDTH)

def _layer(x, c, w_ada, b_ada, w_in, w_pool_grp, pool_scale, sinks, w_pool_up, w_attn_up, w_out, ln_g, ln_b):
    mod = jax.nn.silu(c) @ w_ada + b_ada
    shift, scale, gate = jnp.split(mod, 3, axis=-1)
    u = x * (1 + scale[:, None, :]) + shift[:, None, :]
    h = u @ w_in
    p_in, p_gate, q, k, v, a_gate, g_merge = jnp.split(
        h, [OFF_PGATE, OFF_Q, OFF_K, OFF_V, OFF_AGATE, OFF_MERGE], axis=-1)
    y_pool = _pool_mixer(p_in, w_pool_grp, pool_scale) * jax.nn.silu(p_gate)
    y_attn = _sliding_window_attention(q, k, v, sinks) * jax.nn.silu(a_gate)
    g_pool, g_attn = jnp.split(jax.nn.sigmoid(g_merge), N_BRANCHES, axis=-1)
    merged = g_pool * (y_pool @ w_pool_up) + g_attn * (y_attn @ w_attn_up)
    out = merged @ w_out
    return _layernorm(DEEPNORM_ALPHA * x + gate[:, None, :] * out, ln_g, ln_b)

def setup_inputs(seed: int = 0) -> dict:
    key = jax.random.key(seed)
    ks = jax.random.split(key, 14)
    D = D_MODEL
    f32 = jnp.float32
    nrm = lambda k, shape, s: jax.random.normal(k, shape, f32) * s
    col_scale = jnp.ones((N_IN,), f32).at[OFF_V:OFF_AGATE].set(DEEPNORM_BETA)
    return {
        "x": nrm(ks[0], (BATCH, SEQ, D), 1.0),
        "c": nrm(ks[1], (BATCH, D), 1.0),
        "w_ada": nrm(ks[2], (DEPTH, D, 3 * D), D ** -0.5),
        "b_ada": nrm(ks[3], (DEPTH, 3 * D), 0.02),
        "w_in": nrm(ks[4], (DEPTH, D, N_IN), D ** -0.5) * col_scale,
        "w_pool_grp": nrm(ks[5], (DEPTH, POOL_GROUPS, POOL_GROUP_DIM, POOL_GROUP_DIM), POOL_GROUP_DIM ** -0.5),
        "pool_scale": 1.0 + nrm(ks[6], (DEPTH, POOL_WIDTH), 0.1),
        "sinks": nrm(ks[7], (DEPTH, N_Q_HEADS), 1.0),
        "w_pool_up": nrm(ks[8], (DEPTH, POOL_WIDTH, D), POOL_WIDTH ** -0.5 * DEEPNORM_BETA),
        "w_attn_up": nrm(ks[9], (DEPTH, ATTN_WIDTH, D), ATTN_WIDTH ** -0.5 * DEEPNORM_BETA),
        "w_out": nrm(ks[10], (DEPTH, D, D), D ** -0.5 * DEEPNORM_BETA),
        "ln_g": 1.0 + nrm(ks[11], (DEPTH, D), 0.05),
        "ln_b": nrm(ks[12], (DEPTH, D), 0.02),
    }

def reference(x, c, w_ada, b_ada, w_in, w_pool_grp, pool_scale, sinks, w_pool_up, w_attn_up, w_out, ln_g, ln_b):
    for l in range(DEPTH):
        x = _layer(x, c, w_ada[l], b_ada[l], w_in[l], w_pool_grp[l], pool_scale[l], sinks[l],
                   w_pool_up[l], w_attn_up[l], w_out[l], ln_g[l], ln_b[l])
    return x


_drawn_inputs = setup_inputs


def setup_inputs(seed=0):
    import zlib

    import numpy as np

    out = dict(_drawn_inputs(seed))
    spreads = {}
    factors = {'b_ada': 8.0, 'pool_scale': 6.125, 'sinks': 8.0, 'ln_b': 2.909}
    for name, (base, spread) in spreads.items():
        noise = np.random.default_rng([zlib.crc32(name.encode()), seed]).standard_normal(out[name].shape)
        drawn = base * np.exp(spread * noise) if base else spread * noise
        out[name] = __import__('jax').numpy.asarray(drawn.astype(out[name].dtype))
    for name, factor in factors.items():
        out[name] = (out[name] * factor).astype(out[name].dtype)
    return out
```

```python
from contextlib import ExitStack

import concourse.bass as bass
from concourse import mybir

F32 = mybir.dt.float32
F32R = mybir.dt.float32r
ALU = mybir.AluOpType
ACT = mybir.ActivationFunctionType
AX = mybir.AxisListType

P = 128
D = 2048
S = 1024
NK = D // P
POOL_WINDOWS = (2, 4, 8, 16)
PAD = 16
PW = 1024
AW = 1024
KVW = 256
HD = 64
BLK = 128
NB = S // BLK
QG = 4
OFF_PGATE = PW
OFF_Q = 2 * PW
OFF_K = OFF_Q + AW
OFF_V = OFF_K + KVW
OFF_AGATE = OFF_V + KVW
OFF_MERGE = OFF_AGATE + AW
ALPHA = 2.0 ** 0.25
EPS = 1e-5
MASKED = -1e30

GC = 256
HS = S // 2
NPAIR = 8
RING = 4
G_V, G_PIN, G_SILU, G_Q, G_MERGE, G_UP, G_OUT, G_END = 1, 2, 6, 14, 18, 34, 42, 58
READ_UP = 4 * G_MERGE + 4
PASSES = ((0, 0), (0, 1), (1, 0))


def hybrid_layer(nc, x, c, w_ada, b_ada, w_in, w_pool_grp, pool_scale, sinks,
                 w_pool_up, w_attn_up, w_out, ln_g, ln_b, out):
    with ExitStack() as ctx:
        def sb(name, shape, dt=F32):
            return ctx.enter_context(nc.sbuf_tensor(name, shape, dt))

        def sem(name):
            return ctx.enter_context(nc.semaphore(name))

        def scratch(name, shape):
            return nc.dram_tensor(name, shape, F32, kind="Internal").ap()

        d_k = scratch("d_k", (KVW, S))
        d_v = scratch("d_v", (S, KVW))
        d_p = scratch("d_p", (PW, S))
        d_silu = scratch("d_silu", (PW + AW, S))
        d_q = scratch("d_q", (AW, S))
        d_tanh = scratch("d_tanh", (2 * D, S))
        d_y = scratch("d_y", (PW + AW, S))
        d_m = scratch("d_m", (D, S))
        d_gate = scratch("d_gate", (NK, P))

        act = sb("act", [P, 2, NK, S], F32R)
        wraw = sb("wraw", [P, RING, 2, GC])
        wsp = sb("wsp", [P, RING, 2, 2, GC], F32R)
        ident = sb("ident", [P, P])
        ones = sb("ones", [P, 1])
        mask = sb("mask", [P, 2 * BLK])
        csb = sb("csb", [P, 16])
        ctanh = sb("ctanh", [P, 16])
        bias_mod = sb("bias_mod", [P, NK, 2])
        bias_gate = sb("bias_gate", [P, NK])
        mod = sb("mod", [P, NK, 2])
        gcol = sb("gcol", [P, NK])
        pscale = sb("pscale", [P, 8])
        sink = sb("sink", [P, 16])
        corr = sb("corr", [P, 4, 16])
        small = sb("small", [P, 8, 4])
        stats = sb("stats", [P, 4, 4, 6])
        mv = sb("mv", [P, 4, 2])
        lnc = sb("lnc", [P, 8, 4])
        W1 = sb("W1", [P, 8256])
        with nc.sbuf_tensor("R2", [P, 5120], F32) as R2:
            pass
        with nc.sbuf_tensor("pooled", [P, 2, 2, S], F32R) as pooled, \
                nc.sbuf_tensor("wg", [P, 2, 2, 256], F32R) as wg:
            pass
        with nc.sbuf_tensor("qs", [P, 2, QG * BLK], F32R) as qs, \
                nc.sbuf_tensor("ks", [P, 2, 2 * BLK], F32R) as ks, \
                nc.sbuf_tensor("vz", [P, 2, 2, 2, P], F32R) as vz, \
                nc.sbuf_tensor("pt", [P, 2, 2, QG * BLK], F32R) as pt:
            pass

        adab = W1[:, 0:8192].rearrange("p (b s t d) -> p b s t d", b=2, s=2, t=16)
        xb = R2[:, 0:2048].rearrange("p (b t d) -> p b t d", b=2, t=8)
        u32 = R2[:, 2048:3072]
        acc = R2[:, 3072:3584].rearrange("p (b s d) -> p b s d", b=2, s=2)
        rows = R2[:, 3584:3968].rearrange("p (a d) -> p a d", a=3)
        stage = W1[:, 0:2048].rearrange("p (b n) -> p b n", b=4)
        stage0 = R2[:, 3072:5120].rearrange("p (b n) -> p b n", b=4)
        tanhb = W1[:, 2048:4096].rearrange("p (b n) -> p b n", b=4)
        adag = W1[:, 4096:8192].rearrange("p (b t d) -> p b t d", b=2, t=16)
        PB = PAD + S
        praw = W1[:, 2048:2048 + 2 * PB].rearrange("p (c n) -> p c n", c=2)
        win = [W1[:, 2048 + (2 + n) * PB:2048 + (3 + n) * PB] for n in range(2)]
        psilu = W1[:, 2048 + 4 * PB:].rearrange("p (b n) -> p b n", b=4)
        wgraw = psilu[:, 0, :].rearrange("p (c n) -> p c n", c=2)
        qraw = W1[:, 2048:2560].rearrange("p (g n) -> p g n", g=QG)
        kraw = W1[:, 2560:2816]
        vraw = W1[:, 2816:3072].rearrange("p (h n) -> p h n", h=2)
        asilu = W1[:, 3072:3584].rearrange("p (g n) -> p g n", g=QG)
        yst = W1[:, 3584:4096].rearrange("p (g n) -> p g n", g=QG)
        prob = W1[:, 4096:6144].rearrange("p (h g n) -> p h g n", h=2, g=QG)
        tgate = [W1[:, 2048 * n:2048 * n + 2048].rearrange("p (t n) -> p t n", t=2) for n in range(2)]
        yraw = W1[:, 6144:8192].rearrange("p (b n) -> p b n", b=2)
        z = W1[:, 0:8192].rearrange("p (t n) -> p t n", t=4)
        gateb = R2[:, 0:2048]
        xres = R2[:, 2048:3072].rearrange("p (t n) -> p t n", t=4)
        lngb = R2[:, 3072:5120].rearrange("p (b s n) -> p b s n", b=2, s=2)
        mraw = R2[:, 3072:5120].rearrange("p (b n) -> p b n", b=2)

        ps = ctx.enter_context(nc.psum_tensor("ps", [P, 8, 512], F32))

        pool_steps = sem("pool_steps")
        dve_steps = sem("dve_steps")
        setup_in = sem("setup_in")
        consts = sem("consts")
        ones_made = sem("ones_made")
        cols_t = sem("cols_t")
        cols_c = sem("cols_c")
        c_tanh = sem("c_tanh")
        w_landed = [sem(f"w_landed{n}") for n in range(RING)]
        w_hi = sem("w_hi")
        w_lo = sem("w_lo")
        w_used = sem("w_used")
        x_landed = [sem(f"x_landed{n}") for n in range(2)]
        ada_landed = [sem(f"ada_landed{n}") for n in range(2)]
        x_turned = sem("x_turned")
        ada_mult = sem("ada_mult")
        acc_made = sem("acc_made")
        mod_done = sem("mod_done")
        mod_made = sem("mod_made")
        u_made = sem("u_made")
        a_hi = sem("a_hi")
        a_lo = sem("a_lo")
        gemm_done = sem("gemm_done")
        dve_read = sem("dve_read")
        act_read = sem("act_read")
        tanh_made = sem("tanh_made")
        stored = [sem(f"stored{n}") for n in range(4)]
        agate_landed = [sem(f"agate_landed{n}") for n in range(2)]
        gmult = sem("gmult")
        gmod_done = sem("gmod_done")
        gcol_made = sem("gcol_made")
        grow_t = sem("grow_t")
        grow_c = sem("grow_c")
        grow_stored = sem("grow_stored")
        p_landed = sem("p_landed")
        wg_landed = sem("wg_landed")
        ps_landed = sem("ps_landed")
        chain = sem("chain")
        win_made = sem("win_made")
        pooled_hi = sem("pooled_hi")
        pooled_lo = sem("pooled_lo")
        wg_hi = sem("wg_hi")
        wg_lo = sem("wg_lo")
        mix_done = sem("mix_done")
        mix_read = sem("mix_read")
        ypool_stored = sem("ypool_stored")
        vz_zeroed = sem("vz_zeroed")
        q_landed = sem("q_landed")
        asilu_landed = sem("asilu_landed")
        qkv_hi = sem("qkv_hi")
        qkv_lo = sem("qkv_lo")
        qk_done = sem("qk_done")
        max_made = sem("max_made")
        neg_made = sem("neg_made")
        dsink_made = sem("dsink_made")
        exp_made = sem("exp_made")
        den_made = sem("den_made")
        rden_made = sem("rden_made")
        prob_made = sem("prob_made")
        turned = sem("turned")
        pt_hi = sem("pt_hi")
        pt_lo = sem("pt_lo")
        pv_done = sem("pv_done")
        yatt_made = sem("yatt_made")
        yatt_stored = sem("yatt_stored")
        tg_landed = [sem(f"tg_landed{n}") for n in range(2)]
        m_made = sem("m_made")
        m_stored = sem("m_stored")
        fill_landed = [sem(f"fill_landed{n}") for n in range(2)]
        gateb_landed = sem("gateb_landed")
        xres_landed = sem("xres_landed")
        zg_made = sem("zg_made")
        z_made = sem("z_made")
        stats_made = sem("stats_made")
        var_made = sem("var_made")
        std_made = sem("std_made")
        lnc_made = sem("lnc_made")
        zn_made = sem("zn_made")
        lngb_landed = [sem(f"lngb_landed{n}") for n in range(2)]
        zg2_made = sem("zg2_made")
        zb_made = sem("zb_made")
        out_stored = sem("out_stored")

        def wait(eng, s, value):
            if not isinstance(value, int) or value > 0:
                eng.wait_ge(s, value)

        ada_v = w_ada[0].rearrange("(t p) n -> p t n", p=P)
        x_v = x[0].rearrange("(t p) d -> p t d", p=P)
        out_v = out[0].rearrange("(t p) d -> p t d", p=P)
        w_v = [w.rearrange("(k p) n -> p k n", p=P) for w in (w_in[0], w_pool_up[0], w_attn_up[0], w_out[0])]
        IN, PUP, AUP, OUT = range(4)

        block = ctx.enter_context(nc.Block())

        @block.sync
        def _(sp):
            def load_pair(g, j, which, col, k0):
                wait(sp, w_lo, NPAIR * g + j - RING + 1)
                sp.dma_start(wraw[:, j % RING], w_v[which][:, k0:k0 + 2, bass.ds(col, GC)]).then_inc(
                    w_landed[j % RING], 16)

            sp.dma_start(rows[0:16, 0, :], c[0].rearrange("(t p) -> t p", p=P)).then_inc(setup_in, 16)
            sp.dma_start(rows[0:48, 1, :], b_ada[0].rearrange("(t p) -> t p", p=P)).then_inc(setup_in, 16)
            sp.dma_start(rows[0:8, 2, :], pool_scale[0].rearrange("(t p) -> t p", p=P)).then_inc(setup_in, 16)
            sp.dma_start(sink[:], sinks[0].partition_broadcast(P)).then_inc(setup_in, 16)
            for k in range(NK):
                wait(sp, x_turned, k - 1)
                sp.dma_start(xb[:, k % 2], x_v[:, :, k * P:(k + 1) * P]).then_inc(x_landed[k % 2], 16)
                wait(sp, acc_made, 2 * (k - 1))
                for s, off in ((0, D), (1, 0)):
                    sp.dma_start(adab[:, k % 2, s], ada_v[:, :, off + k * P:off + (k + 1) * P]).then_inc(
                        ada_landed[k % 2], 16)
                if k % 2 == 0:
                    load_pair(0, k // 2, IN, OFF_K, k)
            for j in range(NPAIR):
                load_pair(G_V, j, IN, OFF_V, 2 * j)
            with sp.Fori(0, 4) as i:
                for j in range(NPAIR):
                    load_pair(i + G_PIN, j, IN, i * GC, 2 * j)
            sp.wait_ge(acc_made, 2 * NK)
            for part, off in ((0, OFF_PGATE), (1, OFF_AGATE)):
                with sp.Fori(0, 4) as i:
                    for j in range(NPAIR):
                        load_pair(i + (G_SILU + 4 * part), j, IN, i * GC + off, 2 * j)
                        if j % 4 == 1:
                            m = j // 4
                            sp.wait_ge(acc_made, 2 * i + (2 * NK + 8 * part + m - 1))
                            sp.dma_start(adag[:, m], ada_v[:, :, bass.ds(i * GC + (2 * D + (8 * part + m) * P), P)]
                                         ).then_inc(agate_landed[m], 16)
            with sp.Fori(0, 4) as i:
                for j in range(NPAIR):
                    load_pair(i + G_Q, j, IN, i * GC + OFF_Q, 2 * j)
            with sp.Fori(0, 16) as i:
                for j in range(NPAIR):
                    load_pair(i + G_MERGE, j, IN, i * GC + OFF_MERGE, 2 * j)
            with sp.Fori(0, 8) as i:
                for j in range(NPAIR):
                    load_pair(i + G_UP, j, PUP if j < 4 else AUP, i * GC, 2 * (j % 4))
            for h in range(2):
                with sp.Fori(0, 8) as i:
                    for j in range(NPAIR):
                        load_pair(i + (G_OUT + 8 * h), j, OUT, i * GC, 2 * j)
            sp.wait_ge(out_stored, 16 * 8)

        @block.gpsimd
        def _(pool):
            def start(dst, src):
                pool.sem_inc(pool_steps, 1)
                return pool.dma_start(dst, src)

            nc.gpsimd.memset(ident[:], 0.0).then_inc(consts, 1)
            nc.gpsimd.memset(mask[:], 0.0).then_inc(consts, 1)
            pool.wait_ge(consts, 2)
            nc.gpsimd.affine_select(out=ident[:], in_=ident[:], compare_op=ALU.not_equal, fill=1.0, base=0,
                                    pattern=[[-1, P]], channel_multiplier=1).then_inc(consts, 1)
            nc.gpsimd.affine_select(out=mask[:, 0:BLK], in_=mask[:, 0:BLK], compare_op=ALU.is_gt, fill=MASKED,
                                    base=0, pattern=[[1, BLK]], channel_multiplier=-1).then_inc(consts, 1)
            nc.gpsimd.affine_select(out=mask[:, BLK:], in_=mask[:, BLK:], compare_op=ALU.is_ge, fill=MASKED,
                                    base=0, pattern=[[-1, BLK]], channel_multiplier=1).then_inc(consts, 1)
            for t in range(16):
                nc.gpsimd.memset(corr[:, :, t], float(t + 1)).then_inc(consts, 1)

            def store_banks(g, dst, row, ready, count, src=stage):
                for b in range(4):
                    t, h = b // 2, b % 2
                    pool.wait_ge(ready, count + b + 1)
                    start(dst[bass.ds(row + t * P, P), h * HS:(h + 1) * HS], src[:, b]).then_inc(stored[b], 16)

            store_banks(0, d_k, 0, dve_read, 0, stage0)
            for b in range(4):
                pool.wait_ge(dve_read, 4 + 2 * b + 2)
                start(d_v[2 * b * P:(2 * b + 2) * P, :].rearrange("(t p) n -> p t n", p=P),
                               stage[:, b].rearrange("p (t n) -> p t n", t=2)).then_inc(stored[b], 16)
            with pool.Fori(0, 4) as i:
                store_banks(None, d_p, i * GC, dve_read, (i + G_PIN) * 4 + 4)
            with pool.Fori(0, 8) as i:
                store_banks(None, d_silu, i * GC, dve_read, (i + G_SILU) * 4 + 4)
            pool.wait_ge(grow_c, 1)
            start(d_gate[:, :], rows[0:16, 0, :]).then_inc(grow_stored, 16)

            with pool.Fori(0, 4) as i:
                pool.wait_ge(dve_read, (i + G_Q) * 4 + 4)
                for b in range(4):
                    pool.wait_ge(stored[b], 16 * G_Q)
                start(praw[:, :, PAD:], d_p[bass.ds(i * GC, GC), :].rearrange("(c p) n -> p c n", p=P)
                               ).then_inc(p_landed, 16)
                start(wgraw, w_pool_grp[0].rearrange("g r n -> (g r) n")[bass.ds(i * GC, GC), :]
                               .rearrange("(c p) n -> p c n", p=P)).then_inc(wg_landed, 16)
                pool.wait_ge(wg_lo, i + 1)
                start(psilu.rearrange("p (t h) n -> p t (h n)", t=2),
                               d_silu[bass.ds(i * GC, GC), :].rearrange("(t p) n -> p t n", p=P)
                               ).then_inc(ps_landed, 16)
                for b in range(4):
                    t, h = b // 2, b % 2
                    pool.wait_ge(mix_read, i * 4 + (b + 1))
                    start(d_y[bass.ds(i * GC + t * P, P), h * HS:(h + 1) * HS], psilu[:, b]
                                   ).then_inc(ypool_stored, 16)
                store_banks(None, d_q, i * GC, dve_read, (i + G_Q) * 4 + 4)
                pool.wait_ge(ypool_stored, i * 64 + 64)

            def load_qkv(n, p, it):
                wait(pool, qkv_lo, it)
                first = isinstance(n, int) and n == 0
                for par in range(2):
                    src = d_q[(2 * p + par) * QG * HD:(2 * p + par + 1) * QG * HD, bass.ds(n * BLK, BLK)]
                    start(qraw[par * HD:(par + 1) * HD], src.rearrange("(g d) n -> d g n", d=HD)
                                   ).then_inc(q_landed, 16)
                if first:
                    start(kraw[:, BLK:], d_k[p * P:(p + 1) * P, 0:BLK]).then_inc(q_landed, 16)
                    start(vraw[:, 1], d_v[0:BLK, p * P:(p + 1) * P]).then_inc(q_landed, 16)
                else:
                    start(kraw, d_k[p * P:(p + 1) * P, bass.ds((n - 1) * BLK, 2 * BLK)]
                                   ).then_inc(q_landed, 16)
                    start(vraw, d_v[bass.ds((n - 1) * BLK, 2 * BLK), p * P:(p + 1) * P]
                                   .rearrange("(h k) n -> k h n", h=2)).then_inc(q_landed, 16)

            def load_asilu(n, p, it):
                wait(pool, yatt_made, it)
                for par in range(2):
                    r = PW + (2 * p + par) * QG * HD
                    start(asilu[par * HD:(par + 1) * HD],
                                   d_silu[r:r + QG * HD, bass.ds(n * BLK, BLK)].rearrange("(g d) n -> d g n", d=HD)
                                   ).then_inc(asilu_landed, 16)

            def store_yatt(n, p, it):
                pool.wait_ge(yatt_made, it + 1)
                for par in range(2):
                    r = PW + (2 * p + par) * QG * HD
                    start(d_y[r:r + QG * HD, bass.ds(n * BLK, BLK)].rearrange("(g d) n -> d g n", d=HD),
                                   yst[par * HD:(par + 1) * HD]).then_inc(yatt_stored, 16)

            for b in range(4):
                pool.wait_ge(stored[b], 16 * G_MERGE)
            load_qkv(0, 0, 0)
            load_asilu(0, 0, 0)

            def merge_group(n, p, it, after):
                if after is not None:
                    load_qkv(*after)
                store_yatt(n, p, it)
                if after is not None:
                    load_asilu(*after)
                store_banks(None, d_tanh, it * GC, act_read, it * 4)

            merge_group(0, 0, 0, (0, 1, 1))
            merge_group(0, 1, 1, (1, 0, 2))
            with pool.Fori(1, NB - 1) as n:
                merge_group(n, 0, 2 * n, (n, 1, 2 * n + 1))
                merge_group(n, 1, 2 * n + 1, (n + 1, 0, 2 * n + 2))
            merge_group(NB - 1, 0, 2 * NB - 2, (NB - 1, 1, 2 * NB - 1))

            def load_fill(f, src, raw):
                wait(pool, a_lo, f - 1)
                start(raw[:, f % 2], src[(f % NK) * P:(f % NK + 1) * P, :]).then_inc(fill_landed[f % 2], 16)

            pool.wait_ge(ypool_stored, 16 * 16)
            load_fill(NK, d_y, yraw)
            load_fill(NK + 1, d_y, yraw)
            merge_group(NB - 1, 1, 2 * NB - 1, None)
            for f in range(NK + 2, 2 * NK):
                if f == NK + 6:
                    for b in range(4):
                        pool.wait_ge(stored[b], 16 * G_UP)
                    pool.wait_ge(yatt_stored, 16 * 2 * 2 * NB)
                    for which in range(2):
                        start(tgate[which], d_tanh[which * D:which * D + GC, :]
                                       .rearrange("(t p) n -> p t n", p=P)).then_inc(tg_landed[which], 16)
                load_fill(f, d_y, yraw)

            def up_stores(i, load_next):
                for t in range(2):
                    pool.wait_ge(m_made, i * 4 + 2 * t + 2)
                    start(d_m[bass.ds(i * GC + t * P, P), :], tgate[1][:, t]).then_inc(m_stored, 16)
                if load_next:
                    start(tgate[0], d_tanh[bass.ds(i * GC + GC, GC), :].rearrange("(t p) n -> p t n", p=P)
                                   ).then_inc(tg_landed[0], 16)
                    pool.wait_ge(m_stored, i * 32 + 32)
                    start(tgate[1], d_tanh[bass.ds(i * GC + (D + GC), GC), :]
                                   .rearrange("(t p) n -> p t n", p=P)).then_inc(tg_landed[1], 16)

            with pool.Fori(0, 7) as i:
                up_stores(i, True)
            pool.wait_ge(grow_stored, 16)
            start(gateb, d_gate.rearrange("t p -> (t p)").partition_broadcast(P)
                           ).then_inc(gateb_landed, 16)
            for f in range(2 * NK, 3 * NK):
                if f == 2 * NK:
                    pool.wait_ge(m_stored, 7 * 32)
                if f == 3 * NK - 2:
                    up_stores(7, False)
                    pool.wait_ge(m_stored, 8 * 32)
                load_fill(f, d_m, mraw)
            pool.wait_ge(a_lo, 3 * NK)

            def load_xres(h, i, o):
                wait(pool, z_made, 4 * o)
                start(xres, x_v[:, 4 * h:4 * h + 4, bass.ds(i * GC, GC)]).then_inc(xres_landed, 16)

            def load_lngb(h, cc):
                wait(pool, zb_made, (4 * h + cc - 1) * 4)
                for s, src in ((0, ln_g), (1, ln_b)):
                    start(lngb[:, cc % 2, s], src[0, cc * 512:(cc + 1) * 512].partition_broadcast(P)
                                   ).then_inc(lngb_landed[cc % 2], 16)

            def store_out(h, cc):
                pool.wait_ge(zb_made, (4 * h + cc + 1) * 4)
                start(out_v[:, 4 * h:4 * h + 4, cc * 512:(cc + 1) * 512], z[:, :, cc * 512:(cc + 1) * 512]
                               ).then_inc(out_stored, 16)

            for h in range(2):
                if h == 0:
                    load_xres(h, 0, 0)
                with pool.Fori(1, 8) as i:
                    load_xres(h, i, i + 8 * h)
                load_lngb(h, 0)
                if h == 0:
                    load_xres(1, 0, 8)
                for cc in range(4):
                    if cc < 3:
                        load_lngb(h, cc + 1)
                    store_out(h, cc)

        @block.tensor
        def _(pe):
            def product(dst, stat, mov, first, last, done=None, start=None):
                for n, (a, b) in enumerate(PASSES):
                    mm = nc.tensor.matmul(dst, stat(a), mov(b), start=first and n == 0, stop=last and n == 2)
                    if n == 0 and start is not None:
                        mm.then_inc(start, 1)
                if done is not None:
                    mm.then_inc(done, 1)

            def begin_pair(g, j):
                pe.wait_ge(w_lo, NPAIR * g + j + 1)

            def group_rows(g, reuse, nk=NK, j0=0, kt0=0, bank0=0, hooks=None, fill0=None):
                for k in range(nk):
                    j = j0 + k // 2
                    if k % 2 == 0:
                        begin_pair(g, j)
                    if hooks and k in hooks:
                        hooks[k]()
                    if fill0 is not None:
                        pe.wait_ge(a_lo, fill0 + kt0 + k + 1)
                    for b in range(4):
                        t, h = b // 2, b % 2
                        if k == 0:
                            reuse(b)
                        product(ps[:, bank0 + b, :],
                                lambda a: wsp[:, j % RING, a, k % 2, t * P:(t + 1) * P],
                                lambda a: act[:, a, kt0 + k, h * HS:(h + 1) * HS],
                                k == 0, k == nk - 1,
                                done=gemm_done if k == nk - 1 else None,
                                start=w_used if k % 2 == 0 and b == 0 else None)

            pe.wait_ge(consts, 5)
            pe.wait_ge(setup_in, 64)
            nc.tensor.transpose(ps[:, 7, 0:16], rows[0:16, 0, :], ident[0:16, 0:16])
            nc.tensor.transpose(ps[:, 7, 64:112], rows[0:48, 1, :], ident[0:48, 0:48])
            nc.tensor.transpose(ps[:, 7, 128:136], rows[0:8, 2, :], ident[0:8, 0:8]).then_inc(cols_t, 1)

            for k in range(NK + 1):
                if k < NK:
                    pe.wait_ge(x_landed[k % 2], 16 * (k // 2 + 1))
                    wait(pe, u_made, k)
                    for t in range(8):
                        mm = nc.tensor.transpose(ps[:, 4 + t // 4, (t % 4) * P:(t % 4 + 1) * P], xb[:, k % 2, t, :],
                                                 ident[:])
                    mm.then_inc(x_turned, 1)
                    pe.wait_ge(acc_made, 2 * k + 2)
                    if k == 0:
                        pe.wait_ge(ones_made, 1)
                    for s in range(2):
                        mm = nc.tensor.matmul(ps[:, 6, s:s + 1], acc[:, k % 2, s, :], ones[:], start=True, stop=True)
                    mm.then_inc(mod_done, 1)
                if k >= 1:
                    kt = k - 1
                    j = kt // 2
                    if kt % 2 == 0:
                        begin_pair(0, j)
                    pe.wait_ge(a_lo, kt + 1)
                    for b in range(4):
                        t, h = b // 2, b % 2
                        product(ps[:, b, :],
                                lambda a: wsp[:, j % RING, a, kt % 2, t * P:(t + 1) * P],
                                lambda a: act[:, a, kt, h * HS:(h + 1) * HS],
                                kt == 0, kt == NK - 1, done=gemm_done if kt == NK - 1 else None,
                                start=w_used if kt and kt % 2 == 0 and b == 0 else None)

            for k in range(NK):
                if k % 2 == 0:
                    begin_pair(G_V, k // 2)
                for t in range(8):
                    if k == 0 and t < 4:
                        pe.wait_ge(dve_read, t + 1)
                    product(ps[:, t, 0:GC],
                            lambda a: act[:, a, k, t * P:(t + 1) * P],
                            lambda a: wsp[:, (k // 2) % RING, a, k % 2, :],
                            k == 0, k == NK - 1, done=gemm_done if k == NK - 1 else None,
                            start=w_used if k % 2 == 0 and t == 0 else None)

            def after_dve(g):
                return lambda b: pe.wait_ge(dve_read, g * 4 + (b + 1))

            with pe.Fori(0, 4) as i:
                group_rows(i + G_PIN, after_dve(i + G_PIN))

            with pe.Fori(0, 8) as i:
                def gate_chunk(m):
                    def go():
                        pe.wait_ge(acc_made, 2 * i + (2 * NK + m + 1))
                        nc.tensor.matmul(ps[:, 6, m:m + 1], acc[:, m, 0, :], ones[:], start=True, stop=True
                                         ).then_inc(gmod_done, 1)
                    return go
                group_rows(i + G_SILU, after_dve(i + G_SILU), hooks={9: gate_chunk(0)})
                gate_chunk(1)()
            pe.wait_ge(gcol_made, 17)
            nc.tensor.transpose(ps[0:16, 7, 0:P], gcol[:], ident[:]).then_inc(grow_t, 1)

            with pe.Fori(0, 4) as i:
                def mixer():
                    pe.wait_ge(wg_lo, i + 1)
                    pe.wait_ge(pooled_lo, 2 * i + 2)
                    for b in range(4):
                        t, h = b // 2, b % 2
                        for kc in range(2):
                            product(ps[:, 4 + b, :],
                                    lambda a: wg[:, a, kc, t * P:(t + 1) * P],
                                    lambda a: pooled[:, a, kc, h * HS:(h + 1) * HS],
                                    kc == 0, kc == 1, done=mix_done if kc else None)
                group_rows(i + G_Q, after_dve(i + G_Q), hooks={12: mixer})

            def merge_group(n, p, it, reuse):
                first = isinstance(n, int) and n == 0
                halves = (1,) if first else (0, 1)
                keys = slice(BLK, 2 * BLK) if first else slice(0, 2 * BLK)

                def tidx(par, hf):
                    return 2 * it + par if first else 4 * it - 4 + (2 * par + hf)

                def scores(par):
                    def go():
                        if par == 0:
                            pe.wait_ge(qkv_lo, it + 1)
                        wait(pe, max_made, 2 * it + par)
                        rows_ = slice(par * HD, (par + 1) * HD)
                        for g in range(QG):
                            off = (g % 2) * 2 * BLK
                            product(ps[:, 4 + g // 2, off + keys.start:off + keys.stop],
                                    lambda a: qs[rows_, a, g * BLK:(g + 1) * BLK],
                                    lambda a: ks[rows_, a, keys], True, True,
                                    done=qk_done if g == QG - 1 else None)
                    return go

                def turn(par, hf):
                    def go():
                        pe.wait_ge(prob_made, 2 * it + par + 1)
                        wait(pe, pt_lo, tidx(par, hf))
                        for g in range(QG):
                            mm = nc.tensor.transpose(ps[:, 6, g * BLK:(g + 1) * BLK],
                                                     prob[:, par, g, hf * BLK:(hf + 1) * BLK], ident[:])
                        mm.then_inc(turned, 1)
                    return go

                def pv(par):
                    def go():
                        if par == 0:
                            wait(pe, yatt_made, it)
                        for hf in halves:
                            pe.wait_ge(pt_lo, tidx(par, hf) + 1)
                            product(ps[:, 7, :], lambda a: vz[:, a, par, hf, :], lambda a: pt[:, hf, a, :],
                                    par == 0 and hf == halves[0], par == 1 and hf == 1, done=pv_done)
                    return go

                def both(*f):
                    return lambda: [g() for g in f]
                hooks = {2: scores(0), 6: scores(1), 11: pv(0)}
                if first:
                    hooks |= {9: turn(0, 1), 13: turn(1, 1)}
                else:
                    hooks |= {8: turn(0, 0), 9: turn(0, 1), 12: turn(1, 0), 13: turn(1, 1)}
                group_rows(it + G_MERGE, reuse, hooks=hooks)
                pv(1)()

            def after_act(it):
                return lambda b: pe.wait_ge(act_read, it * 4 + (b - 3))

            pe.wait_ge(mix_read, 16)
            merge_group(0, 0, 0, after_dve(G_MERGE))
            merge_group(0, 1, 1, after_act(1))
            with pe.Fori(1, NB) as n:
                merge_group(n, 0, 2 * n, after_act(2 * n))
                merge_group(n, 1, 2 * n + 1, after_act(2 * n + 1))

            def up_group(i, reuse_a, reuse_b, fill):
                group_rows(i + G_UP, reuse_a, nk=8, fill0=fill)
                group_rows(i + G_UP, reuse_b, nk=8, j0=4, kt0=8, bank0=4, fill0=fill)

            up_group(0, lambda b: pe.wait_ge(act_read, 61 + b), lambda b: pe.wait_ge(yatt_made, 2 * NB), NK)
            with pe.Fori(1, 8) as i:
                up_group(i, lambda b: pe.wait_ge(dve_read, i * 8 + (READ_UP - 8 + b + 1)),
                         lambda b: pe.wait_ge(dve_read, i * 8 + (READ_UP - 4 + b + 1)), None)

            def out_group(h, o, st, fill):
                for k in range(NK):
                    if k % 2 == 0:
                        begin_pair(o + G_OUT, k // 2)
                    if fill:
                        pe.wait_ge(a_lo, 2 * NK + k + 1)
                    for t in range(4):
                        if k == 0:
                            pe.wait_ge(dve_read, o * 4 + (READ_UP + 57 + t))
                        product(ps[:, 4 * st + t, 0:GC],
                                lambda a: act[:, a, k, h * HS + t * P:h * HS + (t + 1) * P],
                                lambda a: wsp[:, (k // 2) % RING, a, k % 2, :],
                                k == 0, k == NK - 1, done=gemm_done if k == NK - 1 else None,
                                start=w_used if k % 2 == 0 and t == 0 else None)

            for h in range(2):
                if h == 0:
                    out_group(0, 0, 0, True)
                    out_group(0, 1, 1, False)
                with pe.Fori(1 - h, 4) as i:
                    out_group(h, 2 * i + 8 * h, 0, False)
                    out_group(h, 2 * i + (8 * h + 1), 1, False)

        @block.scalar
        def _(act_e):
            def hi_pair(g, i):
                s = i % RING
                act_e.wait_ge(w_landed[s], g * (16 * NPAIR // RING) + 16 * (i // RING + 1))
                wait(act_e, w_used, g * NPAIR + (i - RING + 1))
                nc.scalar.copy(wsp[:, s, 0].rearrange("p k n -> p (k n)"),
                               wraw[:, s].rearrange("p k n -> p (k n)")).then_inc(w_hi, 1)

            def group(g, hooks=None, last=False):
                for i in range(NPAIR):
                    if not last or i + 3 < NPAIR:
                        hi_pair(g, i + 3)
                    if hooks and i in hooks:
                        hooks[i]()

            act_e.wait_ge(cols_t, 1)
            nc.scalar.activation(ctanh[:], ps[:, 7, 0:16], ACT.Tanh, scale=0.5).then_inc(c_tanh, 1)
            hi_pair(0, 0)
            act_e.wait_ge(cols_c, 6)
            for k in range(NK + 1):
                if k < NK:
                    act_e.wait_ge(ada_landed[k % 2], 32 * (k // 2 + 1))
                    for s in range(2):
                        for t in range(16):
                            ins = nc.scalar.activation(adab[:, k % 2, s, t, :], adab[:, k % 2, s, t, :], ACT.Identity,
                                                       scale=csb[:, t:t + 1])
                        ins.then_inc(ada_mult, 1)
                if k >= 1:
                    act_e.wait_ge(u_made, k)
                    nc.scalar.copy(act[:, 0, k - 1, :], u32).then_inc(a_hi, 1)
                if k % 2 == 1:
                    hi_pair(0, k // 2 + 1)
            for i in range(NPAIR + 1, NPAIR + 3):
                hi_pair(0, i)
            group(G_V)
            with act_e.Fori(0, 4) as i:
                group(i + G_PIN)

            with act_e.Fori(0, 8) as i:
                def gate_mult(m):
                    def go():
                        act_e.wait_ge(agate_landed[m], i * 16 + 16)
                        for t in range(16):
                            ins = nc.scalar.activation(adag[:, m, t, :], adag[:, m, t, :], ACT.Identity,
                                                       scale=csb[:, t:t + 1])
                        ins.then_inc(gmult, 1)
                    return go
                group(i + G_SILU, {2: gate_mult(0), 5: gate_mult(1)})
                for b in range(4):
                    act_e.wait_ge(gemm_done, (i + G_SILU) * 4 + (5 + b))
                    act_e.wait_ge(dve_read, (i + G_SILU) * 4 + (b + 1))
                    nc.scalar.activation(tanhb[:, b], ps[:, b, :], ACT.Tanh, scale=0.5).then_inc(tanh_made, 1)

            with act_e.Fori(0, 4) as i:
                def split_wg():
                    act_e.wait_ge(wg_landed, i * 16 + 16)
                    nc.scalar.copy(wg[:, 0].rearrange("p c n -> p (c n)"),
                                   wgraw.rearrange("p c n -> p (c n)")).then_inc(wg_hi, 1)

                def split_pooled(kc):
                    def go():
                        act_e.wait_ge(win_made, 2 * i + (kc + 1))
                        nc.scalar.copy(pooled[:, 0, kc, :], win[1][:, PAD:]).then_inc(pooled_hi, 1)
                    return go
                group(i + G_Q, {0: split_wg, 2: split_pooled(0), 4: split_pooled(1)})

            def merge_group(n, p, it):
                first = isinstance(n, int) and n == 0
                hfs = slice(1, 2) if first else slice(0, 2)
                keys = slice(BLK, 2 * BLK) if first else slice(0, 2 * BLK)

                def tidx(par, hf):
                    return 2 * it + par if first else 4 * it - 4 + (2 * par + hf)

                def split_qkv():
                    act_e.wait_ge(q_landed, it * 64 + 64)
                    if not first or it:
                        act_e.wait_ge(pv_done, 2 * it if first else 4 * it - 4)
                    nc.scalar.copy(qs[:, 0], qraw.rearrange("p g n -> p (g n)"))
                    nc.scalar.copy(ks[:, 0, keys], kraw[:, keys])
                    for par in range(2):
                        cs = slice(par * HD, (par + 1) * HD)
                        ins = nc.scalar.copy(vz[:, 0, par, hfs, cs], vraw[:, hfs, cs])
                    ins.then_inc(qkv_hi, 1)

                def exps(par):
                    act_e.wait_ge(neg_made, 2 * it + par + 1)
                    for g in range(QG):
                        nc.scalar.activation(prob[:, par, g, keys], prob[:, par, g, keys], ACT.Exp,
                                             bias=small[:, 4 * par + 1, g:g + 1],
                                             accum_out=small[:, 4 * par + 2, g:g + 1])
                    act_e.wait_ge(dsink_made, 2 * it + par + 1)
                    nc.scalar.activation(small[:, 4 * par + 3], small[:, 4 * par + 3], ACT.Exp).then_inc(exp_made, 1)

                def pt_split(par, hf):
                    if first and hf == 0:
                        return
                    act_e.wait_ge(turned, tidx(par, hf) + 1)
                    if first:
                        wait(act_e, pv_done, tidx(par, hf))
                    else:
                        wait(act_e, pv_done, tidx(par, hf) - 1)
                    nc.scalar.copy(pt[:, hf, 0], ps[:, 6, :]).then_inc(pt_hi, 1)

                def two(*f):
                    return lambda: [g() for g in f]
                group(it + G_MERGE, {
                    0: split_qkv,
                    2: lambda: exps(0),
                    4: lambda: (pt_split(0, 0), exps(1)),
                    5: lambda: pt_split(0, 1),
                    6: lambda: pt_split(1, 0),
                    7: lambda: pt_split(1, 1)})
                for b in range(4):
                    act_e.wait_ge(gemm_done, it * 4 + (4 * G_MERGE + 5 + b))
                    act_e.wait_ge(stored[b], it * 16 + 16 * G_MERGE)
                    nc.scalar.activation(stage[:, b], ps[:, b, :], ACT.Tanh, scale=0.5).then_inc(act_read, 1)

            act_e.wait_ge(vz_zeroed, 1)
            merge_group(0, 0, 0)
            merge_group(0, 1, 1)
            with act_e.Fori(1, NB) as n:
                merge_group(n, 0, 2 * n)
                merge_group(n, 1, 2 * n + 1)

            def fill_hi(f, raw, last_user):
                act_e.wait_ge(fill_landed[f % 2], 16 * (f // 2 - NK // 2 + 1))
                act_e.wait_ge(w_used, NPAIR * last_user + (f % NK) // 2 + 1)
                nc.scalar.copy(act[:, 0, f % NK, :], raw[:, f % 2]).then_inc(a_hi, 1)

            for f in range(NK, NK + 4):
                fill_hi(f, yraw, G_UP - 1)
            group(G_UP, {i: (lambda i=i: [fill_hi(NK + 4 + 2 * i + e, yraw, G_UP - 1) for e in range(2)])
                         for i in range(6)})
            with act_e.Fori(1, 8) as i:
                group(i + G_UP)
            for f in range(2 * NK, 2 * NK + 8):
                fill_hi(f, mraw, G_OUT - 1)
            group(G_OUT, {i: (lambda i=i: fill_hi(2 * NK + 8 + i, mraw, G_OUT - 1)) for i in range(8)})
            for h in range(2):
                with act_e.Fori(1 - h, 8 - h) as i:
                    group(i + (G_OUT + 8 * h))
                if h == 1:
                    group(G_END - 1, last=True)
                act_e.wait_ge(var_made, h + 1)
                nc.scalar.activation(lnc[:, 1], lnc[:, 0], ACT.Sqrt).then_inc(std_made, 1)
                act_e.wait_ge(lnc_made, h + 1)
                for t in range(4):
                    nc.scalar.activation(z[:, t], z[:, t], ACT.Identity, scale=lnc[:, 4, t:t + 1],
                                         bias=lnc[:, 5, t:t + 1]).then_inc(zn_made, 1)

        @block.vector
        def _(dve):
            links = [0]

            def link(ins):
                links[0] += 1
                ins.then_inc(chain, 1)
                dve.wait_ge(chain, links[0])

            def lo_pair(g, i):
                s = i % RING
                dve.wait_ge(w_hi, g * NPAIR + (i + 1))
                nc.vector.tensor_tensor(wsp[:, s, 1], wraw[:, s], wsp[:, s, 0].bitcast(F32),
                                        ALU.subtract).then_inc(w_lo, 1)

            def group(g, hooks=None, last=False):
                for i in range(NPAIR):
                    if not last or i + 3 < NPAIR:
                        lo_pair(g, i + 3)
                    if hooks and i in hooks:
                        hooks[i]()

            nc.vector.memset(ones[:], 1.0).then_inc(ones_made, 1)
            dve.wait_ge(c_tanh, 1)
            nc.vector.scalar_tensor_tensor(csb[:], ctanh[:], 1.0, ps[:, 7, 0:16], ALU.add, ALU.mult).then_inc(cols_c, 1)
            dve.wait_ge(cols_c, 1)
            nc.vector.tensor_scalar(csb[:], csb[:], 0.5, None, ALU.mult).then_inc(cols_c, 1)
            nc.vector.tensor_scalar(bias_mod[:, :, 0], ps[:, 7, 80:96], 1.0, None, ALU.add).then_inc(cols_c, 1)
            nc.vector.tensor_copy(bias_mod[:, :, 1], ps[:, 7, 64:80]).then_inc(cols_c, 1)
            nc.vector.tensor_copy(bias_gate[:], ps[:, 7, 96:112]).then_inc(cols_c, 1)
            nc.vector.tensor_scalar(pscale[:], ps[:, 7, 128:136], 0.5, None, ALU.mult).then_inc(cols_c, 1)
            dve.wait_ge(cols_c, 6)
            dve.wait_ge(consts, 21)
            link(nc.vector.reciprocal(corr[:], corr[:]))
            for g, w in enumerate(POOL_WINDOWS):
                nc.vector.tensor_scalar(corr[:, g], corr[:, g], float(w), 1.0, ALU.mult, ALU.max)

            lo_pair(0, 0)
            for k in range(NK + 1):
                if k < NK:
                    for s in range(2):
                        dve.wait_ge(ada_mult, 2 * k + s + 1)
                        nc.vector.tensor_reduce(acc[:, k % 2, s, :], adab[:, k % 2, s].rearrange("p t d -> p d t"),
                                                AX.X, ALU.add).then_inc(acc_made, 1)
                if k >= 1:
                    dve.wait_ge(a_hi, k)
                    nc.vector.tensor_tensor(act[:, 1, k - 1, :], u32, act[:, 0, k - 1, :].bitcast(F32),
                                            ALU.subtract).then_inc(a_lo, 1)
                if k < NK:
                    dve.wait_ge(mod_done, k + 1)
                    nc.vector.tensor_tensor(mod[:, k, :], ps[:, 6, 0:2], bias_mod[:, k, :], ALU.add).then_inc(mod_made, 1)
                    dve.wait_ge(mod_made, k + 1)
                    dve.wait_ge(x_turned, k + 1)
                    for h in range(2):
                        ins = nc.vector.tensor_scalar(u32[:, h * HS:(h + 1) * HS], ps[:, 4 + h, :], mod[:, k, 0:1],
                                                      mod[:, k, 1:2], ALU.mult, ALU.add)
                    ins.then_inc(u_made, 1)
                if k % 2 == 1:
                    lo_pair(0, k // 2 + 1)
            for i in range(NPAIR + 1, NPAIR + 3):
                lo_pair(0, i)
            for b in range(4):
                dve.wait_ge(gemm_done, b + 1)
                nc.vector.tensor_copy(stage0[:, b], ps[:, b, :]).then_inc(dve_read, 1)
            group(G_V)
            for t in range(8):
                dve.wait_ge(gemm_done, 4 + t + 1)
                nc.vector.tensor_copy(stage[:, t // 2, (t % 2) * GC:(t % 2 + 1) * GC], ps[:, t, 0:GC]
                                      ).then_inc(dve_read, 1)

            def copy_banks(g):
                for b in range(4):
                    dve.wait_ge(gemm_done, g * 4 + (5 + b))
                    dve.wait_ge(stored[b], g * 16)
                    nc.vector.tensor_copy(stage[:, b], ps[:, b, :]).then_inc(dve_read, 1)

            with dve.Fori(0, 4) as i:
                group(i + G_PIN)
                copy_banks(i + G_PIN)

            with dve.Fori(0, 8) as i:
                def gate_sum(m):
                    dve.wait_ge(gmult, 2 * i + (m + 1))
                    nc.vector.tensor_reduce(acc[:, m, 0, :], adag[:, m].rearrange("p t d -> p d t"),
                                            AX.X, ALU.add).then_inc(acc_made, 1)

                def gate_col(m):
                    dve.wait_ge(gmod_done, 2 * i + (m + 1))
                    nc.vector.tensor_tensor(gcol[:, bass.ds(2 * i + m, 1)], ps[:, 6, m:m + 1],
                                            bias_gate[:, bass.ds(2 * i + m, 1)], ALU.add).then_inc(gcol_made, 1)
                group(i + G_SILU, {3: lambda: gate_sum(0), 6: lambda: (gate_col(0), gate_sum(1))})
                for b in range(4):
                    dve.wait_ge(tanh_made, i * 4 + (b + 1))
                    dve.wait_ge(stored[b], (i + G_SILU) * 16)
                    nc.vector.scalar_tensor_tensor(stage[:, b], tanhb[:, b], 1.0, ps[:, b, :], ALU.add, ALU.mult
                                                   ).then_inc(dve_read, 1)
                gate_col(1)
            dve.wait_ge(gcol_made, 16)
            nc.vector.tensor_scalar(gcol[:], gcol[:], 0.5, None, ALU.mult).then_inc(gcol_made, 1)
            nc.vector.memset(praw[:, :, 0:PAD], 0.0)
            dve.wait_ge(grow_t, 1)
            nc.vector.tensor_copy(rows[0:16, 0, :], ps[0:16, 7, 0:P]).then_inc(grow_c, 1)

            for g, w in enumerate(POOL_WINDOWS):
                def wg_split():
                    dve.wait_ge(wg_hi, g + 1)
                    nc.vector.tensor_tensor(wg[:, 1], wgraw, wg[:, 0].bitcast(F32), ALU.subtract).then_inc(wg_lo, 1)

                def pool_window(kc):
                    dve.wait_ge(p_landed, 16 * (g + 1))
                    wait(dve, pooled_lo, 2 * g + kc)
                    src, width, n = praw[:, kc], 1, g
                    while width < w:
                        dst = win[1] if n % 2 == 0 else win[0]
                        lo = 2 * width - 1
                        link(nc.vector.tensor_tensor(dst[:, lo:], src[:, lo:], src[:, lo - width:PB - width], ALU.add))
                        src, width, n = dst, 2 * width, n - 1
                    link(nc.vector.tensor_tensor(src[:, PAD:2 * PAD], src[:, PAD:2 * PAD], corr[:, g], ALU.mult))
                    nc.vector.scalar_tensor_tensor(win[1][:, PAD:], src[:, PAD:], 1.0 / w, praw[:, kc, PAD:],
                                                   ALU.mult, ALU.subtract).then_inc(win_made, 1)

                def pooled_split(kc):
                    dve.wait_ge(pooled_hi, 2 * g + kc + 1)
                    nc.vector.tensor_tensor(pooled[:, 1, kc], win[1][:, PAD:], pooled[:, 0, kc].bitcast(F32),
                                            ALU.subtract).then_inc(pooled_lo, 1)

                def mixed():
                    dve.wait_ge(ps_landed, 16 * (g + 1))
                    for b in range(4):
                        dve.wait_ge(mix_done, 4 * g + b + 1)
                        nc.vector.scalar_tensor_tensor(psilu[:, b], ps[:, 4 + b, :],
                                                       pscale[:, 2 * g + b // 2:2 * g + b // 2 + 1], psilu[:, b],
                                                       ALU.mult, ALU.mult).then_inc(mix_read, 1)
                group(g + G_Q, {0: wg_split, 1: lambda: pool_window(0),
                                3: lambda: (pooled_split(0), pool_window(1)),
                                5: lambda: pooled_split(1), 7: mixed})
                copy_banks(g + G_Q)

            nc.vector.memset(vz[:].bitcast(F32), 0.0).then_inc(vz_zeroed, 1)

            def merge_group(n, p, it):
                first = isinstance(n, int) and n == 0
                hfs = slice(1, 2) if first else slice(0, 2)
                keys = slice(BLK, 2 * BLK) if first else slice(0, 2 * BLK)

                def tidx(par, hf):
                    return 2 * it + par if first else 4 * it - 4 + (2 * par + hf)

                def qkv_split():
                    dve.wait_ge(qkv_hi, it + 1)
                    nc.vector.tensor_tensor(qs[:, 1], qraw.rearrange("p g n -> p (g n)"), qs[:, 0].bitcast(F32),
                                            ALU.subtract)
                    nc.vector.tensor_tensor(ks[:, 1, keys], kraw[:, keys], ks[:, 0, keys].bitcast(F32), ALU.subtract)
                    for par in range(2):
                        cs = slice(par * HD, (par + 1) * HD)
                        ins = nc.vector.tensor_tensor(vz[:, 1, par, hfs, cs], vraw[:, hfs, cs],
                                                      vz[:, 0, par, hfs, cs].bitcast(F32), ALU.subtract)
                    ins.then_inc(qkv_lo, 1)

                def maxima(par):
                    dve.wait_ge(qk_done, 2 * it + par + 1)
                    dve.sem_inc(dve_steps, 1)
                    for g in range(QG):
                        off = (g % 2) * 2 * BLK
                        hd = (2 * p + par) * QG + g
                        ins = nc.vector.tensor_tensor_reduce(
                            out=prob[:, par, g, keys], in0=ps[:, 4 + g // 2, off + keys.start:off + keys.stop],
                            in1=mask[:, keys], scale=HD ** -0.5, scalar=sink[:, hd:hd + 1], op0=ALU.add,
                            op1=ALU.max, accum_out=small[:, 4 * par, g:g + 1])
                    ins.then_inc(max_made, 1)
                    dve.wait_ge(max_made, 2 * it + par + 1)
                    nc.vector.tensor_scalar(small[:, 4 * par + 1], small[:, 4 * par], -1.0, None, ALU.mult
                                            ).then_inc(neg_made, 1)
                    h0 = (2 * p + par) * QG
                    nc.vector.tensor_tensor(small[:, 4 * par + 3], sink[:, h0:h0 + QG], small[:, 4 * par],
                                            ALU.subtract).then_inc(dsink_made, 1)

                def normalise(par):
                    dve.wait_ge(exp_made, 2 * it + par + 1)
                    nc.vector.tensor_tensor(small[:, 4 * par + 2], small[:, 4 * par + 2], small[:, 4 * par + 3],
                                            ALU.add).then_inc(den_made, 1)
                    dve.wait_ge(den_made, 2 * it + par + 1)
                    nc.vector.reciprocal(small[:, 4 * par + 2], small[:, 4 * par + 2]).then_inc(rden_made, 1)
                    dve.wait_ge(rden_made, 2 * it + par + 1)
                    for g in range(QG):
                        ins = nc.vector.tensor_scalar(prob[:, par, g, keys], prob[:, par, g, keys],
                                                      small[:, 4 * par + 2, g:g + 1], None, ALU.mult)
                    ins.then_inc(prob_made, 1)

                def pt_split(par, hf):
                    if first and hf == 0:
                        return
                    dve.wait_ge(pt_hi, tidx(par, hf) + 1)
                    nc.vector.tensor_tensor(pt[:, hf, 1], ps[:, 6, :], pt[:, hf, 0].bitcast(F32), ALU.subtract
                                            ).then_inc(pt_lo, 1)

                group(it + G_MERGE, {
                    0: qkv_split,
                    2: lambda: maxima(0),
                    3: lambda: normalise(0),
                    4: lambda: (maxima(1), pt_split(0, 0)),
                    5: lambda: (normalise(1), pt_split(0, 1)),
                    6: lambda: pt_split(1, 0),
                    7: lambda: pt_split(1, 1)})
                dve.wait_ge(pv_done, 2 * it + 2 if first else 4 * it)
                dve.wait_ge(asilu_landed, it * 32 + 32)
                wait(dve, yatt_stored, it * 32)
                nc.vector.scalar_tensor_tensor(yst.rearrange("p g n -> p (g n)"), ps[:, 7, :], 0.5,
                                               asilu.rearrange("p g n -> p (g n)"), ALU.mult, ALU.mult
                                               ).then_inc(yatt_made, 1)

            merge_group(0, 0, 0)
            merge_group(0, 1, 1)
            with dve.Fori(1, NB) as n:
                merge_group(n, 0, 2 * n)
                merge_group(n, 1, 2 * n + 1)

            def fill_lo(f, raw):
                dve.wait_ge(a_hi, f + 1)
                nc.vector.tensor_tensor(act[:, 1, f % NK], raw[:, f % 2], act[:, 0, f % NK].bitcast(F32),
                                        ALU.subtract).then_inc(a_lo, 1)

            def merge_up(i):
                for which in range(2):
                    dve.wait_ge(tg_landed[which], i * 16 + 16)
                    for b in range(4):
                        t, h = b // 2, b % 2
                        cs = slice(h * HS, (h + 1) * HS)
                        dve.wait_ge(gemm_done, i * 8 + (READ_UP + 64 + 4 * which + b + 1))
                        nc.vector.scalar_tensor_tensor(tgate[which][:, t, cs], tgate[which][:, t, cs], 1.0,
                                                       ps[:, 4 * which + b, :], ALU.add, ALU.mult
                                                       ).then_inc(dve_read, 1)
                dve.wait_ge(dve_read, i * 8 + (READ_UP + 8))
                for b in range(4):
                    t, h = b // 2, b % 2
                    cs = slice(h * HS, (h + 1) * HS)
                    nc.vector.tensor_tensor(tgate[1][:, t, cs], tgate[1][:, t, cs], tgate[0][:, t, cs], ALU.add
                                            ).then_inc(m_made, 1)

            for f in range(NK, NK + 4):
                fill_lo(f, yraw)
            group(G_UP, {i: (lambda i=i: [fill_lo(NK + 4 + 2 * i + e, yraw) for e in range(2)]) for i in range(6)})
            merge_up(0)
            with dve.Fori(1, 8) as i:
                group(i + G_UP)
                merge_up(i)
            for f in range(2 * NK, 2 * NK + 8):
                fill_lo(f, mraw)

            def residual(i, o, st):
                cols = bass.ds(i * GC, GC)
                dve.wait_ge(xres_landed, o * 16 + 16)
                for t in range(4):
                    dve.wait_ge(gemm_done, o * 4 + (READ_UP + 128 + t + 1))
                    nc.vector.tensor_tensor(z[:, t, cols], ps[:, 4 * st + t, 0:GC], gateb[:, cols], ALU.mult
                                            ).then_inc(dve_read, 1)
                dve.wait_ge(dve_read, o * 4 + (READ_UP + 68))
                for t in range(4):
                    nc.vector.scalar_tensor_tensor(z[:, t, cols], xres[:, t], ALPHA, z[:, t, cols], ALU.mult, ALU.add
                                                   ).then_inc(z_made, 1)

            def two_groups(h, i, hooks=None, last=False):
                for e in range(2):
                    group(2 * i + (G_OUT + 8 * h + e), hooks if e == 0 else None, last=last and e == 1)
                    if e == 0 and hooks and h == 1:
                        dve.wait_ge(out_stored, 16 * 4)
                    residual(2 * i + e, 2 * i + (8 * h + e), e)
                dve.wait_ge(z_made, i * 8 + (32 * h + 8))
                for t in range(4):
                    ins = nc.vector.bn_stats(stats[:, t, bass.ds(i, 1), :], z[:, t, bass.ds(i * 512, 512)])
                ins.then_inc(stats_made, 1)

            def norm_columns(h):
                dve.wait_ge(stats_made, 4 * (h + 1))
                for t in range(4):
                    ins = nc.vector.bn_aggr(mv[:, t], stats[:, t].rearrange("p a s -> p (a s)"))
                link(ins)
                nc.vector.tensor_scalar(lnc[:, 0], mv[:, :, 1], EPS, None, ALU.add).then_inc(var_made, 1)
                dve.wait_ge(std_made, h + 1)
                link(nc.vector.reciprocal(lnc[:, 2], lnc[:, 1]))
                link(nc.vector.tensor_tensor(lnc[:, 3], lnc[:, 2], lnc[:, 2], ALU.mult))
                link(nc.vector.tensor_tensor(lnc[:, 3], lnc[:, 3], lnc[:, 0], ALU.mult))
                link(nc.vector.tensor_scalar(lnc[:, 3], lnc[:, 3], -0.5, 1.5, ALU.mult, ALU.add))
                link(nc.vector.tensor_tensor(lnc[:, 4], lnc[:, 2], lnc[:, 3], ALU.mult))
                nc.vector.scalar_tensor_tensor(lnc[:, 5], mv[:, :, 0], -1.0, lnc[:, 4], ALU.mult, ALU.mult
                                               ).then_inc(lnc_made, 1)

            def norm_mult(h, cc):
                dve.wait_ge(lngb_landed[cc % 2], 32 * (2 * h + cc // 2 + 1))
                for t in range(4):
                    dve.wait_ge(zn_made, 4 * h + t + 1)
                    cs = slice(cc * 512, (cc + 1) * 512)
                    ins = nc.vector.tensor_tensor(z[:, t, cs], z[:, t, cs], lngb[:, cc % 2, 0], ALU.mult)
                ins.then_inc(zg2_made, 1)

            def norm_add(h, cc):
                dve.wait_ge(zg2_made, 4 * h + cc + 1)
                for t in range(4):
                    cs = slice(cc * 512, (cc + 1) * 512)
                    nc.vector.tensor_tensor(z[:, t, cs], z[:, t, cs], lngb[:, cc % 2, 1], ALU.add
                                            ).then_inc(zb_made, 1)

            dve.wait_ge(gateb_landed, 16)
            two_groups(0, 0, {i: (lambda i=i: fill_lo(2 * NK + 8 + i, mraw)) for i in range(8)})
            with dve.Fori(1, 4) as i:
                two_groups(0, i)
            norm_columns(0)
            two_groups(1, 0, {i: (lambda i=i: (norm_add if i % 2 else norm_mult)(0, i // 2)) for i in range(8)})
            with dve.Fori(1, 3) as i:
                two_groups(1, i)
            two_groups(1, 3, last=True)
            norm_columns(1)
            for cc in range(4):
                norm_mult(1, cc)
                norm_add(1, cc)


_INS = ["x", "c", "w_ada", "b_ada", "w_in", "w_pool_grp", "pool_scale", "sinks", "w_pool_up", "w_attn_up",
        "w_out", "ln_g", "ln_b"]
_OUT = ((1, S, D), "float32")


def kernel(**inputs):
    import numpy as _np
    import concourse.bacc as _bacc
    from concourse import mybir as _mybir
    from concourse.bass_utils import run_bass_kernel_spmd as _run

    nc = _bacc.Bacc("TRN2", target_bir_lowering=False, num_devices=1)
    arrays, args = {}, []
    for name in _INS:
        a = _np.ascontiguousarray(inputs[name])
        arrays[f"in_{name}_dram"] = a
        args.append(nc.dram_tensor(f"in_{name}_dram", a.shape, _mybir.dt.from_np(a.dtype), kind="ExternalInput").ap())
    args.append(nc.dram_tensor("out_0_dram", _OUT[0], _mybir.dt.from_np(_np.dtype(_OUT[1])), kind="ExternalOutput").ap())
    hybrid_layer(nc, *args)
    r = _run(nc, [arrays], core_ids=[0])
    return r.results[0]["out_0_dram"]
```

```python
from contextlib import ExitStack

import concourse.bass as bass
from concourse import mybir

F32 = mybir.dt.float32
F32R = mybir.dt.float32r
ALU = mybir.AluOpType
ACT = mybir.ActivationFunctionType
AX = mybir.AxisListType

P = 128
D = 2048
S = 1024
NK = D // P
POOL_WINDOWS = (2, 4, 8, 16)
PAD = 16
PW = 1024
AW = 1024
KVW = 256
HD = 64
BLK = 128
NB = S // BLK
QG = 4
OFF_PGATE = PW
OFF_Q = 2 * PW
OFF_K = OFF_Q + AW
OFF_V = OFF_K + KVW
OFF_AGATE = OFF_V + KVW
OFF_MERGE = OFF_AGATE + AW
ALPHA = 2.0 ** 0.25
EPS = 1e-5
MASKED = -1e30

GC = 256
HS = S // 2
NPAIR = 8
RING = 4
G_V, G_PIN, G_SILU, G_Q, G_MERGE, G_UP, G_OUT = 1, 2, 6, 14, 18, 34, 42
READ_UP = 4 * G_MERGE
OC = 512
NOUT = 8
DIRECT = 5
PASSES = ((0, 0), (0, 1), (1, 0))


def first_pair(g):
    return NPAIR * g + NPAIR


def first_out(og):
    return first_pair(G_OUT) + NK * og


def hybrid_layer(nc, x, c, w_ada, b_ada, w_in, w_pool_grp, pool_scale, sinks,
                 w_pool_up, w_attn_up, w_out, ln_g, ln_b, out):
    with ExitStack() as ctx:
        def sb(name, shape, dt=F32):
            return ctx.enter_context(nc.sbuf_tensor(name, shape, dt))

        def sem(name):
            return ctx.enter_context(nc.semaphore(name))

        def scratch(name, shape):
            return nc.dram_tensor(name, shape, F32, kind="Internal").ap()

        d_k = scratch("d_k", (KVW, S))
        d_v = scratch("d_v", (S, KVW))
        d_p = scratch("d_p", (PW, S))
        d_silu = scratch("d_silu", (PW + AW, S))
        d_q = scratch("d_q", (AW, S))
        d_tanh = scratch("d_tanh", (2 * D, S))
        d_y = scratch("d_y", (PW + AW, S))
        d_m = scratch("d_m", (D, S))
        d_gate = scratch("d_gate", (NK, P))

        act = sb("act", [P, 2, NK, S], F32R)
        wraw = sb("wraw", [P, RING, 2, GC])
        wsp = sb("wsp", [P, RING, 2, 2, GC], F32R)
        ident = sb("ident", [P, P])
        ones = sb("ones", [P, 1])
        mask = sb("mask", [P, 2 * BLK])
        csb = sb("csb", [P, 16])
        ctanh = sb("ctanh", [P, 16])
        bias_mod = sb("bias_mod", [P, NK, 2])
        bias_gate = sb("bias_gate", [P, NK])
        mod = sb("mod", [P, NK, 2])
        gcol = sb("gcol", [P, NK])
        pscale = sb("pscale", [P, 8])
        sink = sb("sink", [P, 16])
        corr = sb("corr", [P, 4, 16])
        small = sb("small", [P, 8, 4])
        stats = sb("stats", [P, 4, 4, 6])
        mv = sb("mv", [P, 4, 2])
        lnc = sb("lnc", [P, 8, 4])
        W1 = sb("W1", [P, 8256])
        with nc.sbuf_tensor("R2", [P, 5120], F32) as R2:
            pass
        with nc.sbuf_tensor("pooled", [P, 2, 2, S], F32R) as pooled, \
                nc.sbuf_tensor("wg", [P, 2, 2, 256], F32R) as wg:
            pass
        with nc.sbuf_tensor("qs", [P, 2, QG * BLK], F32R) as qs, \
                nc.sbuf_tensor("ks", [P, 2, 2 * BLK], F32R) as ks, \
                nc.sbuf_tensor("vz", [P, 2, 2, 2, P], F32R) as vz, \
                nc.sbuf_tensor("pt", [P, 2, 2, QG * BLK], F32R) as pt:
            pass

        adab = W1[:, 0:8192].rearrange("p (b s t d) -> p b s t d", b=2, s=2, t=16)
        xb = R2[:, 0:2048].rearrange("p (b t d) -> p b t d", b=2, t=8)
        u32 = R2[:, 2048:3072]
        acc = R2[:, 3072:3584].rearrange("p (b s d) -> p b s d", b=2, s=2)
        rows = R2[:, 3584:3968].rearrange("p (a d) -> p a d", a=3)
        stage = W1[:, 0:2048].rearrange("p (b n) -> p b n", b=4)
        stage0 = R2[:, 3072:5120].rearrange("p (b n) -> p b n", b=4)
        tanhb = W1[:, 2048:4096].rearrange("p (b n) -> p b n", b=4)
        adag = W1[:, 4096:8192].rearrange("p (b t d) -> p b t d", b=2, t=16)
        PB = PAD + S
        praw = W1[:, 2048:2048 + 2 * PB].rearrange("p (c n) -> p c n", c=2)
        win = [W1[:, 2048 + (2 + n) * PB:2048 + (3 + n) * PB] for n in range(2)]
        psilu = W1[:, 2048 + 4 * PB:].rearrange("p (b n) -> p b n", b=4)
        wgraw = psilu[:, 0, :].rearrange("p (c n) -> p c n", c=2)
        qraw = W1[:, 2048:2560].rearrange("p (g n) -> p g n", g=QG)
        kraw = W1[:, 2560:2816]
        vraw = W1[:, 2816:3072].rearrange("p (h n) -> p h n", h=2)
        asilu = W1[:, 3072:3584].rearrange("p (g n) -> p g n", g=QG)
        yst = W1[:, 3584:4096].rearrange("p (g n) -> p g n", g=QG)
        prob = W1[:, 4096:6144].rearrange("p (h g n) -> p h g n", h=2, g=QG)
        tgate = [W1[:, 2048 * n:2048 * n + 2048].rearrange("p (t n) -> p t n", t=2) for n in range(2)]
        yraw = W1[:, 6144:8192].rearrange("p (b n) -> p b n", b=2)
        z = W1[:, 0:8192].rearrange("p (t n) -> p t n", t=4)
        gateb = R2[:, 0:2048]
        lateraw = R2[:, 2048:3072].rearrange("p (b n) -> p b n", b=2)
        g_all = R2[:, 3072:5120]
        b_all = wraw.rearrange("p s k n -> p (s k n)")
        lngb = R2[:, 3072:5120].rearrange("p (b s n) -> p b s n", b=2, s=2)
        mraw = R2[:, 3072:5120].rearrange("p (b n) -> p b n", b=2)

        ps = ctx.enter_context(nc.psum_tensor("ps", [P, 8, 512], F32))

        pool_steps = sem("pool_steps")
        dve_steps = sem("dve_steps")
        setup_in = sem("setup_in")
        consts = sem("consts")
        ones_made = sem("ones_made")
        cols_t = sem("cols_t")
        cols_c = sem("cols_c")
        c_tanh = sem("c_tanh")
        w_landed = [sem(f"w_landed{n}") for n in range(RING)]
        w_hi = sem("w_hi")
        w_lo = sem("w_lo")
        w_used = sem("w_used")
        x_landed = [sem(f"x_landed{n}") for n in range(2)]
        ada_landed = [sem(f"ada_landed{n}") for n in range(2)]
        x_turned = sem("x_turned")
        ada_mult = sem("ada_mult")
        acc_made = sem("acc_made")
        mod_done = sem("mod_done")
        mod_made = sem("mod_made")
        u_made = sem("u_made")
        a_hi = sem("a_hi")
        a_lo = sem("a_lo")
        gemm_done = sem("gemm_done")
        dve_read = sem("dve_read")
        act_read = sem("act_read")
        tanh_made = sem("tanh_made")
        stored = [sem(f"stored{n}") for n in range(4)]
        agate_landed = [sem(f"agate_landed{n}") for n in range(2)]
        gmult = sem("gmult")
        gmod_done = sem("gmod_done")
        gcol_made = sem("gcol_made")
        grow_t = sem("grow_t")
        grow_c = sem("grow_c")
        grow_stored = sem("grow_stored")
        p_landed = sem("p_landed")
        wg_landed = sem("wg_landed")
        ps_landed = sem("ps_landed")
        chain = sem("chain")
        win_made = sem("win_made")
        pooled_hi = sem("pooled_hi")
        pooled_lo = sem("pooled_lo")
        wg_hi = sem("wg_hi")
        wg_lo = sem("wg_lo")
        mix_done = sem("mix_done")
        mix_read = sem("mix_read")
        ypool_stored = sem("ypool_stored")
        vz_zeroed = sem("vz_zeroed")
        q_landed = sem("q_landed")
        asilu_landed = sem("asilu_landed")
        qkv_hi = sem("qkv_hi")
        qkv_lo = sem("qkv_lo")
        qk_done = sem("qk_done")
        max_made = sem("max_made")
        neg_made = sem("neg_made")
        dsink_made = sem("dsink_made")
        exp_made = sem("exp_made")
        den_made = sem("den_made")
        rden_made = sem("rden_made")
        prob_made = sem("prob_made")
        turned = sem("turned")
        pt_hi = sem("pt_hi")
        pt_lo = sem("pt_lo")
        pv_done = sem("pv_done")
        yatt_made = sem("yatt_made")
        yatt_stored = sem("yatt_stored")
        tg_landed = [sem(f"tg_landed{n}") for n in range(2)]
        m_made = sem("m_made")
        m_stored = sem("m_stored")
        fill_landed = [sem(f"fill_landed{n}") for n in range(2)]
        gateb_landed = sem("gateb_landed")
        x_in_z = [sem(f"x_in_z{n}") for n in range(4)]
        late_landed = [sem(f"late_landed{n}") for n in range(2)]
        late_hi = sem("late_hi")
        late_lo = sem("late_lo")
        gb_all_landed = sem("gb_all_landed")
        zg_made = sem("zg_made")
        z_made = sem("z_made")
        stats_made = sem("stats_made")
        var_made = sem("var_made")
        std_made = sem("std_made")
        lnc_made = sem("lnc_made")
        lngb_landed = [sem(f"lngb_landed{n}") for n in range(2)]
        zg2_made = sem("zg2_made")
        zb_made = sem("zb_made")
        out_stored = [sem(f"out_stored{n}") for n in range(4)]
        tail_stored = sem("tail_stored")

        def wait(eng, s, value):
            if not isinstance(value, int) or value > 0:
                eng.wait_ge(s, value)

        ada_v = w_ada[0].rearrange("(t p) n -> p t n", p=P)
        x_v = x[0].rearrange("(t p) d -> p t d", p=P)
        out_v = out[0].rearrange("(t p) d -> p t d", p=P)
        w_v = [w.rearrange("(k p) n -> p k n", p=P) for w in (w_in[0], w_pool_up[0], w_attn_up[0], w_out[0])]
        IN, PUP, AUP, OUT = range(4)

        block = ctx.enter_context(nc.Block())

        @block.sync
        def _(sp):
            def load(q, slot, dst, src):
                wait(sp, w_lo, q - RING + 1)
                sp.dma_start(dst, src).then_inc(w_landed[slot], 16)

            def load_pair(g, j, which, col, k0):
                load(first_pair(g) + j, j % RING, wraw[:, j % RING], w_v[which][:, k0:k0 + 2, bass.ds(col, GC)])

            sp.dma_start(rows[0:16, 0, :], c[0].rearrange("(t p) -> t p", p=P)).then_inc(setup_in, 16)
            sp.dma_start(rows[0:48, 1, :], b_ada[0].rearrange("(t p) -> t p", p=P)).then_inc(setup_in, 16)
            sp.dma_start(rows[0:8, 2, :], pool_scale[0].rearrange("(t p) -> t p", p=P)).then_inc(setup_in, 16)
            sp.dma_start(sink[:], sinks[0].partition_broadcast(P)).then_inc(setup_in, 16)
            for k in range(NK):
                wait(sp, x_turned, k - 1)
                sp.dma_start(xb[:, k % 2], x_v[:, :, k * P:(k + 1) * P]).then_inc(x_landed[k % 2], 16)
                wait(sp, mod_done, k - 1)
                for s, off in ((0, D), (1, 0)):
                    sp.dma_start(adab[:, k % 2, s], ada_v[:, :, off + k * P:off + (k + 1) * P]).then_inc(
                        ada_landed[k % 2], 16)
                if k % 2 == 0:
                    for n, off in ((k, OFF_K), (k + 1, OFF_V)):
                        load(n, n % RING, wraw[:, n % RING], w_v[IN][:, k:k + 2, off:off + GC])
            for j in range(NPAIR):
                load_pair(G_V, j, IN, OFF_V, 2 * j)
            with sp.Fori(0, 4) as i:
                for j in range(NPAIR):
                    load_pair(i + G_PIN, j, IN, i * GC, 2 * j)
            sp.wait_ge(mod_done, NK)
            for part, off in ((0, OFF_PGATE), (1, OFF_AGATE)):
                with sp.Fori(0, 4) as i:
                    for j in range(NPAIR):
                        load_pair(i + (G_SILU + 4 * part), j, IN, i * GC + off, 2 * j)
                        if j % 4 == 1:
                            m = j // 4
                            sp.wait_ge(acc_made, 2 * i + (2 * NK + 8 * part + m - 1))
                            sp.dma_start(adag[:, m], ada_v[:, :, bass.ds(i * GC + (2 * D + (8 * part + m) * P), P)]
                                         ).then_inc(agate_landed[m], 16)
            with sp.Fori(0, 4) as i:
                for j in range(NPAIR):
                    load_pair(i + G_Q, j, IN, i * GC + OFF_Q, 2 * j)
            with sp.Fori(0, 16) as i:
                for j in range(NPAIR):
                    load_pair(i + G_MERGE, j, IN, i * GC + OFF_MERGE, 2 * j)
            with sp.Fori(0, 8) as i:
                for j in range(NPAIR):
                    load_pair(i + G_UP, j, PUP if j < 4 else AUP, i * GC, 2 * (j % 4))

            def load_out(og, k, c):
                load(first_out(og) + k, k % RING, wraw[:, k % RING].rearrange("p k n -> p (k n)"),
                     w_out[0][k * P:(k + 1) * P, bass.ds(c * OC, OC)])

            with sp.Fori(0, 4) as i:
                for k in range(NK):
                    load_out(i, k, i)
            for chunk in range(3):
                for k in range(NK):
                    load_out(4 + chunk, k, chunk)
                    m = (chunk - 1) * NK + k - 3
                    if 0 <= m < NK:
                        wait(sp, late_lo, m - 1)
                        sp.dma_start(lateraw[:, m % 2], w_out[0][m * P:(m + 1) * P, 3 * OC:]).then_inc(
                            late_landed[m % 2], 16)
            for cc in range(4):
                sp.wait_ge(out_stored[cc], 16)
            sp.wait_ge(tail_stored, 16 * (2 * 3 + 4))

        @block.gpsimd
        def _(pool):
            def start(dst, src):
                pool.sem_inc(pool_steps, 1)
                return pool.dma_start(dst, src)

            nc.gpsimd.memset(ident[:], 0.0).then_inc(consts, 1)
            nc.gpsimd.memset(mask[:], 0.0).then_inc(consts, 1)
            pool.wait_ge(consts, 2)
            nc.gpsimd.affine_select(out=ident[:], in_=ident[:], compare_op=ALU.not_equal, fill=1.0, base=0,
                                    pattern=[[-1, P]], channel_multiplier=1).then_inc(consts, 1)
            nc.gpsimd.affine_select(out=mask[:, 0:BLK], in_=mask[:, 0:BLK], compare_op=ALU.is_gt, fill=MASKED,
                                    base=0, pattern=[[1, BLK]], channel_multiplier=-1).then_inc(consts, 1)
            nc.gpsimd.affine_select(out=mask[:, BLK:], in_=mask[:, BLK:], compare_op=ALU.is_ge, fill=MASKED,
                                    base=0, pattern=[[-1, BLK]], channel_multiplier=1).then_inc(consts, 1)
            for t in range(16):
                nc.gpsimd.memset(corr[:, :, t], float(t + 1)).then_inc(consts, 1)

            def store_banks(dst, row, ready, count, src=stage):
                for b in range(4):
                    t, h = b // 2, b % 2
                    pool.wait_ge(ready, count + b + 1)
                    start(dst[bass.ds(row + t * P, P), h * HS:(h + 1) * HS], src[:, b]).then_inc(stored[b], 16)

            store_banks(d_k, 0, dve_read, 0, stage0)
            for b in range(4):
                pool.wait_ge(dve_read, 4 + b + 1)
                start(d_v[2 * b * P:(2 * b + 2) * P, :].rearrange("(t p) n -> p t n", p=P),
                               stage[:, b].rearrange("p (t n) -> p t n", t=2)).then_inc(stored[b], 16)
            with pool.Fori(0, 4) as i:
                store_banks(d_p, i * GC, dve_read, (i + G_PIN) * 4)
            with pool.Fori(0, 8) as i:
                store_banks(d_silu, i * GC, dve_read, (i + G_SILU) * 4)
            pool.wait_ge(grow_c, 1)
            start(d_gate[:, :], rows[0:16, 0, :]).then_inc(grow_stored, 16)

            def mixer_io(i):
                pool.wait_ge(dve_read, (i + G_Q) * 4)
                for b in range(4):
                    pool.wait_ge(stored[b], 16 * G_Q)
                start(praw[:, :, PAD:], d_p[bass.ds(i * GC, GC), :].rearrange("(c p) n -> p c n", p=P)
                      ).then_inc(p_landed, 16)
                start(wgraw, w_pool_grp[0].rearrange("g r n -> (g r) n")[bass.ds(i * GC, GC), :]
                      .rearrange("(c p) n -> p c n", p=P)).then_inc(wg_landed, 16)
                pool.wait_ge(wg_lo, i + 1)
                start(psilu.rearrange("p (t h) n -> p t (h n)", t=2),
                      d_silu[bass.ds(i * GC, GC), :].rearrange("(t p) n -> p t n", p=P)).then_inc(ps_landed, 16)
                for b in range(4):
                    t, h = b // 2, b % 2
                    pool.wait_ge(mix_read, i * 4 + (b + 1))
                    start(d_y[bass.ds(i * GC + t * P, P), h * HS:(h + 1) * HS], psilu[:, b]).then_inc(ypool_stored, 16)

            with pool.Fori(0, 3) as i:
                mixer_io(i)
                store_banks(d_q, i * GC, dve_read, (i + G_Q) * 4)
                pool.wait_ge(ypool_stored, i * 64 + 64)

            def load_qkv(n, p, it):
                wait(pool, qkv_lo, it)
                first = isinstance(n, int) and n == 0
                for par in range(2):
                    src = d_q[(2 * p + par) * QG * HD:(2 * p + par + 1) * QG * HD, bass.ds(n * BLK, BLK)]
                    start(qraw[par * HD:(par + 1) * HD], src.rearrange("(g d) n -> d g n", d=HD)
                                   ).then_inc(q_landed, 16)
                if first:
                    start(kraw[:, BLK:], d_k[p * P:(p + 1) * P, 0:BLK]).then_inc(q_landed, 16)
                    start(vraw[:, 1], d_v[0:BLK, p * P:(p + 1) * P]).then_inc(q_landed, 16)
                else:
                    start(kraw, d_k[p * P:(p + 1) * P, bass.ds((n - 1) * BLK, 2 * BLK)]
                                   ).then_inc(q_landed, 16)
                    start(vraw, d_v[bass.ds((n - 1) * BLK, 2 * BLK), p * P:(p + 1) * P]
                                   .rearrange("(h k) n -> k h n", h=2)).then_inc(q_landed, 16)

            def load_asilu(n, p, it):
                wait(pool, yatt_made, it)
                for par in range(2):
                    r = PW + (2 * p + par) * QG * HD
                    start(asilu[par * HD:(par + 1) * HD],
                                   d_silu[r:r + QG * HD, bass.ds(n * BLK, BLK)].rearrange("(g d) n -> d g n", d=HD)
                                   ).then_inc(asilu_landed, 16)

            def store_yatt(n, p, it):
                pool.wait_ge(yatt_made, it + 1)
                for par in range(2):
                    r = PW + (2 * p + par) * QG * HD
                    start(d_y[r:r + QG * HD, bass.ds(n * BLK, BLK)].rearrange("(g d) n -> d g n", d=HD),
                                   yst[par * HD:(par + 1) * HD]).then_inc(yatt_stored, 16)

            mixer_io(3)
            pool.wait_ge(win_made, 8)
            load_qkv(0, 0, 0)
            load_asilu(0, 0, 0)
            store_banks(d_q, 3 * GC, dve_read, (3 + G_Q) * 4)
            for b in range(4):
                pool.wait_ge(stored[b], 16 * G_MERGE)

            def merge_group(n, p, it, after):
                if after is not None:
                    load_qkv(*after)
                store_yatt(n, p, it)
                if after is not None:
                    load_asilu(*after)
                store_banks(d_tanh, it * GC, act_read, it * 4)

            merge_group(0, 0, 0, (0, 1, 1))
            merge_group(0, 1, 1, (1, 0, 2))
            with pool.Fori(1, NB - 1) as n:
                merge_group(n, 0, 2 * n, (n, 1, 2 * n + 1))
                merge_group(n, 1, 2 * n + 1, (n + 1, 0, 2 * n + 2))
            merge_group(NB - 1, 0, 2 * NB - 2, (NB - 1, 1, 2 * NB - 1))

            def load_fill(f, src, raw):
                wait(pool, a_lo, f - 1)
                start(raw[:, f % 2], src[(f % NK) * P:(f % NK + 1) * P, :]).then_inc(fill_landed[f % 2], 16)

            pool.wait_ge(ypool_stored, 16 * 16)
            for f in range(NK, NK + 8):
                load_fill(f, d_y, yraw)
            merge_group(NB - 1, 1, 2 * NB - 1, None)
            for b in range(4):
                pool.wait_ge(stored[b], 16 * G_UP)
            pool.wait_ge(yatt_stored, 16 * 2 * 2 * NB)
            load_fill(NK + 8, d_y, yraw)
            load_fill(NK + 9, d_y, yraw)
            for which in range(2):
                start(tgate[which], d_tanh[which * D:which * D + GC, :].rearrange("(t p) n -> p t n", p=P)
                      ).then_inc(tg_landed[which], 16)
            for f in range(NK + 10, 2 * NK):
                load_fill(f, d_y, yraw)

            def up_stores(i, load_next):
                for t in range(2):
                    pool.wait_ge(m_made, i * 4 + 2 * t + 2)
                    start(d_m[bass.ds(i * GC + t * P, P), :], tgate[1][:, t]).then_inc(m_stored, 16)
                if load_next:
                    start(tgate[0], d_tanh[bass.ds(i * GC + GC, GC), :].rearrange("(t p) n -> p t n", p=P)
                                   ).then_inc(tg_landed[0], 16)
                    pool.wait_ge(m_stored, i * 32 + 32)
                    start(tgate[1], d_tanh[bass.ds(i * GC + (D + GC), GC), :]
                                   .rearrange("(t p) n -> p t n", p=P)).then_inc(tg_landed[1], 16)

            with pool.Fori(0, 7) as i:
                up_stores(i, True)
            pool.wait_ge(grow_stored, 16)
            start(gateb, d_gate.rearrange("t p -> (t p)").partition_broadcast(P)
                           ).then_inc(gateb_landed, 16)
            def store_out(cc):
                pool.wait_ge(zb_made, (cc + 1) * 4)
                cols = slice(cc * OC, (cc + 1) * OC)
                start(out_v[:, 0:4, cols], z[:, :, cols]).then_inc(out_stored[cc], 16)
                pool.wait_ge(out_stored[cc], 16)
                start(z[:, :, cols], x_v[:, 4:8, cols]).then_inc(x_in_z[cc], 16)

            pool.wait_ge(m_stored, 7 * 32)
            for f in range(2 * NK, 2 * NK + 10):
                load_fill(f, d_m, mraw)
            up_stores(7, False)
            pool.wait_ge(m_stored, 8 * 32)
            for f in range(2 * NK + 10, 3 * NK):
                load_fill(f, d_m, mraw)
            for c in range(4):
                start(z[:, :, c * OC:(c + 1) * OC], x_v[:, 0:4, c * OC:(c + 1) * OC]).then_inc(x_in_z[c], 16)
            pool.wait_ge(a_lo, 3 * NK)

            for cc in range(4):
                wait(pool, zb_made, (cc - 1) * 4)
                for s, src in ((0, ln_g), (1, ln_b)):
                    start(lngb[:, cc % 2, s], src[0, cc * OC:(cc + 1) * OC].partition_broadcast(P)
                          ).then_inc(lngb_landed[cc % 2], 16)
                if cc:
                    store_out(cc - 1)
            store_out(3)
            start(g_all, ln_g[0].partition_broadcast(P)).then_inc(gb_all_landed, 16)
            pool.wait_ge(w_lo, first_out(NOUT - 1))
            start(b_all, ln_b[0].partition_broadcast(P)).then_inc(gb_all_landed, 16)
            for t in range(4):
                parts = 4 if t == 3 else 2
                for n in range(parts):
                    w = D // parts
                    pool.wait_ge(zb_made, 16 + 4 * t + (n + 1) * 4 // parts)
                    start(out_v[:, 4 + t, n * w:(n + 1) * w], z[:, t, n * w:(n + 1) * w]).then_inc(tail_stored, 16)

        @block.tensor
        def _(pe):
            def product(dst, stat, mov, first, last, done=None, start=None):
                for n, (a, b) in enumerate(PASSES):
                    mm = nc.tensor.matmul(dst, stat(a), mov(b), start=first and n == 0, stop=last and n == 2)
                    if n == 0 and start is not None:
                        mm.then_inc(start, 1)
                if done is not None:
                    mm.then_inc(done, 1)

            def begin_pair(g, j):
                pe.wait_ge(w_lo, first_pair(g) + (j + 1))

            def group_rows(g, reuse, nk=NK, j0=0, kt0=0, bank0=0, hooks=None, fill0=None):
                for k in range(nk):
                    j = j0 + k // 2
                    if k % 2 == 0:
                        begin_pair(g, j)
                    if hooks and k in hooks:
                        hooks[k]()
                    if fill0 is not None:
                        pe.wait_ge(a_lo, fill0 + kt0 + k + 1)
                    for b in range(4):
                        t, h = b // 2, b % 2
                        if k == 0:
                            reuse(b)
                        product(ps[:, bank0 + b, :],
                                lambda a: wsp[:, j % RING, a, k % 2, t * P:(t + 1) * P],
                                lambda a: act[:, a, kt0 + k, h * HS:(h + 1) * HS],
                                k == 0, k == nk - 1,
                                done=gemm_done if k == nk - 1 else None,
                                start=w_used if k % 2 == 0 and b == 0 else None)

            pe.wait_ge(consts, 5)
            pe.wait_ge(setup_in, 64)
            nc.tensor.transpose(ps[:, 7, 0:16], rows[0:16, 0, :], ident[0:16, 0:16])
            nc.tensor.transpose(ps[:, 7, 64:112], rows[0:48, 1, :], ident[0:48, 0:48])
            nc.tensor.transpose(ps[:, 7, 128:136], rows[0:8, 2, :], ident[0:8, 0:8]).then_inc(cols_t, 1)

            def turn_x(k, h):
                for t in range(4):
                    mm = nc.tensor.transpose(ps[:, 4 + h, t * P:(t + 1) * P], xb[:, k % 2, 4 * h + t, :], ident[:])
                return mm

            def v_step(k, t0, bank0, first_start):
                for t in range(4):
                    for n, (a, b) in enumerate(PASSES):
                        slot = first_start[1]
                        mm = nc.tensor.matmul(ps[:, bank0 + t // 2, (t % 2) * GC:(t % 2 + 1) * GC],
                                              act[:, a, k, (t0 + t) * P:(t0 + t + 1) * P],
                                              wsp[:, slot, b, k % 2, :], start=k == 0 and n == 0 and t % 2 == 0,
                                              stop=k == NK - 1 and n == 2, skip_group_check=True)
                        if n == 0 and t == 0 and first_start[0]:
                            mm.then_inc(w_used, 1)
                    if k == NK - 1 and t % 2 == 1:
                        mm.then_inc(gemm_done, 1)

            for k in range(NK + 1):
                if k < NK:
                    pe.wait_ge(x_landed[k % 2], 16 * (k // 2 + 1))
                    wait(pe, u_made, k)
                    turn_x(k, 0)
                    pe.wait_ge(ada_landed[k % 2], 32 * (k // 2 + 1))
                    if k == 0:
                        pe.wait_ge(cols_c, 6)
                    for s in range(2):
                        for t in range(DIRECT):
                            nc.tensor.matmul(ps[:, 5, s:s + 1], adab[:, k % 2, s, t, :], csb[:, t:t + 1],
                                             start=t == 0, stop=False)
                        pe.wait_ge(acc_made, 2 * k + s + 1)
                        if k == 0:
                            pe.wait_ge(ones_made, 1)
                        mm = nc.tensor.matmul(ps[:, 5, s:s + 1], acc[:, k % 2, s, :], ones[:], start=False, stop=True)
                    mm.then_inc(mod_done, 1)
                if k >= 1:
                    kt = k - 1
                    j = kt // 2
                    if kt % 2 == 0:
                        pe.wait_ge(w_lo, 2 * j + 1)
                    pe.wait_ge(a_lo, kt + 1)
                    for b in range(4):
                        t, h = b // 2, b % 2
                        product(ps[:, b, :],
                                lambda a: wsp[:, 2 * j % RING, a, kt % 2, t * P:(t + 1) * P],
                                lambda a: act[:, a, kt, h * HS:(h + 1) * HS],
                                kt == 0, kt == NK - 1, done=gemm_done if kt == NK - 1 else None,
                                start=w_used if kt and kt % 2 == 0 and b == 0 else None)
                        if b == 0 and k < NK:
                            pe.wait_ge(mod_made, k + 1)
                            turn_x(k, 1).then_inc(x_turned, 1)
                    if kt % 2 == 0:
                        pe.wait_ge(w_lo, 2 * j + 2)
                    v_step(kt, 0, 6, (kt % 2 == 1, (2 * j + 1) % RING))
                else:
                    pe.wait_ge(mod_made, 1)
                    turn_x(0, 1).then_inc(x_turned, 1)

            for k in range(NK):
                if k % 2 == 0:
                    begin_pair(G_V, k // 2)
                v_step(k, 4, 4, (k % 2 == 0, (k // 2) % RING))

            def after_dve(g):
                return lambda b: pe.wait_ge(dve_read, g * 4 + (b - 3))

            with pe.Fori(0, 4) as i:
                group_rows(i + G_PIN, after_dve(i + G_PIN))

            with pe.Fori(0, 8) as i:
                def gate_chunk(m):
                    def go():
                        pe.wait_ge(acc_made, 2 * i + (2 * NK + m + 1))
                        nc.tensor.matmul(ps[:, 6, m:m + 1], acc[:, m, 0, :], ones[:], start=True, stop=True
                                         ).then_inc(gmod_done, 1)
                    return go
                group_rows(i + G_SILU, after_dve(i + G_SILU), hooks={9: gate_chunk(0)})
                gate_chunk(1)()
            pe.wait_ge(gcol_made, 17)
            nc.tensor.transpose(ps[0:16, 7, 0:P], gcol[:], ident[:]).then_inc(grow_t, 1)

            with pe.Fori(0, 4) as i:
                def mixer():
                    pe.wait_ge(wg_lo, i + 1)
                    pe.wait_ge(pooled_lo, 2 * i + 2)
                    for b in range(4):
                        t, h = b // 2, b % 2
                        for kc in range(2):
                            product(ps[:, 4 + b, :],
                                    lambda a: wg[:, a, kc, t * P:(t + 1) * P],
                                    lambda a: pooled[:, a, kc, h * HS:(h + 1) * HS],
                                    kc == 0, kc == 1, done=mix_done if kc else None)
                group_rows(i + G_Q, after_dve(i + G_Q), hooks={12: mixer})

            def merge_group(n, p, it, reuse):
                first = isinstance(n, int) and n == 0
                halves = (1,) if first else (0, 1)
                keys = slice(BLK, 2 * BLK) if first else slice(0, 2 * BLK)

                def tidx(par, hf):
                    return 2 * it + par if first else 4 * it - 4 + (2 * par + hf)

                def scores(par):
                    def go():
                        if par == 0:
                            pe.wait_ge(qkv_lo, it + 1)
                        wait(pe, max_made, 2 * it + par)
                        rows_ = slice(par * HD, (par + 1) * HD)
                        for g in range(QG):
                            off = (g % 2) * 2 * BLK
                            product(ps[:, 4 + g // 2, off + keys.start:off + keys.stop],
                                    lambda a: qs[rows_, a, g * BLK:(g + 1) * BLK],
                                    lambda a: ks[rows_, a, keys], True, True,
                                    done=qk_done if g == QG - 1 else None)
                    return go

                def turn(par, hf):
                    def go():
                        pe.wait_ge(prob_made, 2 * it + par + 1)
                        wait(pe, pt_lo, tidx(par, hf))
                        for g in range(QG):
                            mm = nc.tensor.transpose(ps[:, 6, g * BLK:(g + 1) * BLK],
                                                     prob[:, par, g, hf * BLK:(hf + 1) * BLK], ident[:])
                        mm.then_inc(turned, 1)
                    return go

                def pv(par):
                    def go():
                        if par == 0:
                            wait(pe, yatt_made, it)
                        for hf in halves:
                            pe.wait_ge(pt_lo, tidx(par, hf) + 1)
                            product(ps[:, 7, :], lambda a: vz[:, a, par, hf, :], lambda a: pt[:, hf, a, :],
                                    par == 0 and hf == halves[0], par == 1 and hf == 1, done=pv_done)
                    return go

                def both(*f):
                    return lambda: [g() for g in f]
                hooks = {2: scores(0), 5: scores(1), 10: turn(0, 1), 14: turn(1, 1)}
                if first:
                    hooks |= {12: pv(0)}
                else:
                    hooks |= {8: turn(0, 0), 12: both(turn(1, 0), pv(0))}
                group_rows(it + G_MERGE, reuse, hooks=hooks)
                pv(1)()

            def after_act(it):
                return lambda b: pe.wait_ge(act_read, it * 4 + (b - 3))

            pe.wait_ge(mix_read, 16)
            merge_group(0, 0, 0, after_dve(G_MERGE))
            merge_group(0, 1, 1, after_act(1))
            with pe.Fori(1, NB) as n:
                merge_group(n, 0, 2 * n, after_act(2 * n))
                merge_group(n, 1, 2 * n + 1, after_act(2 * n + 1))

            def up_group(i, reuse_a, reuse_b, fill):
                group_rows(i + G_UP, reuse_a, nk=8, fill0=fill)
                group_rows(i + G_UP, reuse_b, nk=8, j0=4, kt0=8, bank0=4, fill0=fill)

            up_group(0, lambda b: pe.wait_ge(act_read, 61 + b), lambda b: pe.wait_ge(yatt_made, 2 * NB), NK)
            with pe.Fori(1, 8) as i:
                up_group(i, lambda b: pe.wait_ge(dve_read, i * 8 + (READ_UP - 8 + b + 1)),
                         lambda b: pe.wait_ge(dve_read, i * 8 + (READ_UP - 4 + b + 1)), None)

            def out_group(og, h, st):
                for k in range(NK):
                    pe.wait_ge(w_lo, first_out(og) + (k + 1))
                    if h == 0:
                        pe.wait_ge(a_lo, 2 * NK + k + 1)
                    for t in range(4):
                        if k == 0:
                            pe.wait_ge(dve_read, og * 4 + (READ_UP + 57 + t))
                        product(ps[:, 4 * st + t, :],
                                lambda a: act[:, a, k, h * HS + t * P:h * HS + (t + 1) * P],
                                lambda a: wsp[:, k % RING, a].rearrange("p k n -> p (k n)"),
                                k == 0, k == NK - 1, done=gemm_done if k == NK - 1 else None,
                                start=w_used if t == 0 else None)

            with pe.Fori(0, 2) as i:
                out_group(2 * i, 0, 0)
                out_group(2 * i + 1, 0, 1)
            for c in range(3):
                out_group(4 + c, 1, c % 2)
            for t in range(4):
                pe.wait_ge(dve_read, (NOUT - 1) * 4 + (READ_UP + 57 + t))
                for k in range(NK):
                    if t == 0:
                        pe.wait_ge(late_lo, k + 1)
                    product(ps[:, 4 + t, :],
                            lambda a: act[:, a, k, HS + t * P:HS + (t + 1) * P],
                            lambda a: act[:, a, k, 0:HS],
                            k == 0, k == NK - 1, done=gemm_done if k == NK - 1 else None)

        @block.scalar
        def _(act_e):
            def hi_pair(q0, i):
                s = i % RING
                act_e.wait_ge(w_landed[s], q0 * (16 // RING) + 16 * (i // RING + 1))
                wait(act_e, w_used, q0 + (i - RING + 1))
                nc.scalar.copy(wsp[:, s, 0].rearrange("p k n -> p (k n)"),
                               wraw[:, s].rearrange("p k n -> p (k n)")).then_inc(w_hi, 1)

            def group(g, hooks=None):
                for i in range(NPAIR):
                    hi_pair(first_pair(g), i + 3)
                    if hooks and i in hooks:
                        hooks[i]()

            def out_group(og, hooks=None, last=False):
                for i in range(NK):
                    if not last or i + 3 < NK:
                        hi_pair(first_out(og), i + 3)
                    if hooks and i in hooks:
                        hooks[i]()

            act_e.wait_ge(cols_t, 1)
            nc.scalar.activation(ctanh[:], ps[:, 7, 0:16], ACT.Tanh, scale=0.5).then_inc(c_tanh, 1)
            for i in range(2):
                hi_pair(0, i)
            act_e.wait_ge(cols_c, 6)
            for k in range(NK + 1):
                if k < NK:
                    act_e.wait_ge(ada_landed[k % 2], 32 * (k // 2 + 1))
                    for s in range(2):
                        for t in range(DIRECT, 16):
                            ins = nc.scalar.activation(adab[:, k % 2, s, t, :], adab[:, k % 2, s, t, :], ACT.Identity,
                                                       scale=csb[:, t:t + 1])
                        ins.then_inc(ada_mult, 1)
                if k >= 1:
                    act_e.wait_ge(u_made, k)
                    nc.scalar.copy(act[:, 0, k - 1, :], u32).then_inc(a_hi, 1)
                if k % 2 == 1:
                    hi_pair(0, k + 1)
                    hi_pair(0, k + 2)
            hi_pair(0, 2 * NPAIR + 2)
            group(G_V)
            with act_e.Fori(0, 4) as i:
                group(i + G_PIN)

            with act_e.Fori(0, 8) as i:
                def gate_mult(m):
                    def go():
                        act_e.wait_ge(agate_landed[m], i * 16 + 16)
                        for t in range(16):
                            ins = nc.scalar.activation(adag[:, m, t, :], adag[:, m, t, :], ACT.Identity,
                                                       scale=csb[:, t:t + 1])
                        ins.then_inc(gmult, 1)
                    return go
                group(i + G_SILU, {2: gate_mult(0), 5: gate_mult(1)})
                for b in range(4):
                    act_e.wait_ge(gemm_done, (i + G_SILU) * 4 + (1 + b))
                    act_e.wait_ge(dve_read, (i + G_SILU) * 4 + (b - 3))
                    nc.scalar.activation(tanhb[:, b], ps[:, b, :], ACT.Tanh, scale=0.5).then_inc(tanh_made, 1)

            with act_e.Fori(0, 4) as i:
                def split_wg():
                    act_e.wait_ge(wg_landed, i * 16 + 16)
                    nc.scalar.copy(wg[:, 0].rearrange("p c n -> p (c n)"),
                                   wgraw.rearrange("p c n -> p (c n)")).then_inc(wg_hi, 1)

                def split_pooled(kc):
                    def go():
                        act_e.wait_ge(win_made, 2 * i + (kc + 1))
                        nc.scalar.copy(pooled[:, 0, kc, :], win[1][:, PAD:]).then_inc(pooled_hi, 1)
                    return go
                group(i + G_Q, {0: split_wg, 2: split_pooled(0), 4: split_pooled(1)})

            def merge_group(n, p, it, extra={}):
                first = isinstance(n, int) and n == 0
                hfs = slice(1, 2) if first else slice(0, 2)
                keys = slice(BLK, 2 * BLK) if first else slice(0, 2 * BLK)

                def tidx(par, hf):
                    return 2 * it + par if first else 4 * it - 4 + (2 * par + hf)

                def split_qkv():
                    act_e.wait_ge(q_landed, it * 64 + 64)
                    if not first or it:
                        act_e.wait_ge(pv_done, 2 * it if first else 4 * it - 4)
                    nc.scalar.copy(qs[:, 0], qraw.rearrange("p g n -> p (g n)"))
                    nc.scalar.copy(ks[:, 0, keys], kraw[:, keys])
                    for par in range(2):
                        cs = slice(par * HD, (par + 1) * HD)
                        ins = nc.scalar.copy(vz[:, 0, par, hfs, cs], vraw[:, hfs, cs])
                    ins.then_inc(qkv_hi, 1)

                def exps(par):
                    act_e.wait_ge(neg_made, 2 * it + par + 1)
                    for g in range(QG):
                        nc.scalar.activation(prob[:, par, g, keys], prob[:, par, g, keys], ACT.Exp,
                                             bias=small[:, 4 * par + 1, g:g + 1],
                                             accum_out=small[:, 4 * par + 2, g:g + 1])
                    act_e.wait_ge(dsink_made, 2 * it + par + 1)
                    nc.scalar.activation(small[:, 4 * par + 3], small[:, 4 * par + 3], ACT.Exp).then_inc(exp_made, 1)

                def pt_split(par, hf):
                    if first and hf == 0:
                        return
                    act_e.wait_ge(turned, tidx(par, hf) + 1)
                    if first:
                        wait(act_e, pv_done, tidx(par, hf))
                    else:
                        wait(act_e, pv_done, tidx(par, hf) - 1)
                    nc.scalar.copy(pt[:, hf, 0], ps[:, 6, :]).then_inc(pt_hi, 1)

                def step(i):
                    return lambda: [f() for f in {
                        0: [split_qkv], 2: [lambda: exps(0)], 3: [lambda: exps(1)],
                        4: [lambda: pt_split(0, 0)], 5: [lambda: pt_split(0, 1)],
                        6: [lambda: pt_split(1, 0)], 7: [lambda: pt_split(1, 1)]}.get(i, []) + extra.get(i, [])]
                group(it + G_MERGE, {i: step(i) for i in range(NPAIR)})
                for b in range(4):
                    act_e.wait_ge(gemm_done, it * 4 + (4 * G_MERGE + 1 + b))
                    act_e.wait_ge(stored[b], it * 16 + 16 * G_MERGE)
                    nc.scalar.activation(stage[:, b], ps[:, b, :], ACT.Tanh, scale=0.5).then_inc(act_read, 1)

            act_e.wait_ge(vz_zeroed, 1)
            merge_group(0, 0, 0)
            merge_group(0, 1, 1)
            with act_e.Fori(1, NB - 1) as n:
                merge_group(n, 0, 2 * n)
                merge_group(n, 1, 2 * n + 1)

            def fill_hi(f, raw, last_user):
                act_e.wait_ge(fill_landed[f % 2], 16 * (f // 2 - NK // 2 + 1))
                act_e.wait_ge(w_used, first_pair(last_user) + (f % NK) // 2 + 1)
                nc.scalar.copy(act[:, 0, f % NK, :], raw[:, f % 2]).then_inc(a_hi, 1)

            def y_fill(f):
                return lambda: fill_hi(f, yraw, G_UP - 1)

            def m_fill(f):
                return lambda: fill_hi(f, mraw, G_OUT - 1)

            merge_group(NB - 1, 0, 2 * NB - 2)
            merge_group(NB - 1, 1, 2 * NB - 1,
                        {i: [y_fill(NK + 2 * i - 8), y_fill(NK + 2 * i - 7)] for i in range(4, 8)})
            group(G_UP, {i: (lambda i=i: (y_fill(NK + 8 + 2 * i)(), y_fill(NK + 9 + 2 * i)())) for i in range(4)})
            with act_e.Fori(1, 7) as i:
                group(i + G_UP)
            group(G_OUT - 1, {i: (lambda i=i: (m_fill(2 * NK + 2 * i - 8)(), m_fill(2 * NK + 2 * i - 7)()))
                              for i in range(4, 8)})

            def square_root(n):
                act_e.wait_ge(var_made, n + 1)
                nc.scalar.activation(lnc[:, 1], lnc[:, 0], ACT.Sqrt).then_inc(std_made, 1)

            def late(k):
                def go():
                    act_e.wait_ge(late_landed[k % 2], 16 * (k // 2 + 1))
                    if k == 0:
                        act_e.wait_ge(w_used, first_out(4))
                    nc.scalar.copy(act[:, 0, k, 0:HS], lateraw[:, k % 2]).then_inc(late_hi, 1)
                return go

            out_group(0, {i: m_fill(2 * NK + 8 + i) for i in range(8)})
            for og in range(1, 4):
                out_group(og)
            out_group(4, {1: lambda: square_root(0)})
            out_group(5, {k: late(k) for k in range(NK)})
            out_group(6, last=True)
            for t in range(4):
                square_root(1 + t)

        @block.vector
        def _(dve):
            links = [0]

            def link(ins):
                links[0] += 1
                ins.then_inc(chain, 1)
                dve.wait_ge(chain, links[0])

            def lo_pair(q0, i):
                s = i % RING
                dve.wait_ge(w_hi, q0 + (i + 1))
                nc.vector.tensor_tensor(wsp[:, s, 1], wraw[:, s], wsp[:, s, 0].bitcast(F32),
                                        ALU.subtract).then_inc(w_lo, 1)

            def group(g, hooks=None):
                for i in range(NPAIR):
                    lo_pair(first_pair(g), i + 3)
                    if hooks and i in hooks:
                        hooks[i]()

            def out_group(og, hooks=None, last=False):
                for i in range(NK):
                    if not last or i + 3 < NK:
                        lo_pair(first_out(og), i + 3)
                    if hooks and i in hooks:
                        hooks[i]()

            nc.vector.memset(ones[:], 1.0).then_inc(ones_made, 1)
            dve.wait_ge(c_tanh, 1)
            nc.vector.scalar_tensor_tensor(csb[:], ctanh[:], 1.0, ps[:, 7, 0:16], ALU.add, ALU.mult).then_inc(cols_c, 1)
            dve.wait_ge(cols_c, 1)
            nc.vector.tensor_scalar(csb[:], csb[:], 0.5, None, ALU.mult).then_inc(cols_c, 1)
            nc.vector.tensor_scalar(bias_mod[:, :, 0], ps[:, 7, 80:96], 1.0, None, ALU.add).then_inc(cols_c, 1)
            nc.vector.tensor_copy(bias_mod[:, :, 1], ps[:, 7, 64:80]).then_inc(cols_c, 1)
            nc.vector.tensor_copy(bias_gate[:], ps[:, 7, 96:112]).then_inc(cols_c, 1)
            nc.vector.tensor_scalar(pscale[:], ps[:, 7, 128:136], 0.5, None, ALU.mult).then_inc(cols_c, 1)
            dve.wait_ge(cols_c, 6)
            dve.wait_ge(consts, 21)
            link(nc.vector.reciprocal(corr[:], corr[:]))
            for g, w in enumerate(POOL_WINDOWS):
                nc.vector.tensor_scalar(corr[:, g], corr[:, g], float(w), 1.0, ALU.mult, ALU.max)

            for i in range(2):
                lo_pair(0, i)
            for k in range(NK + 1):
                if k < NK:
                    for s in range(2):
                        dve.wait_ge(ada_mult, 2 * k + s + 1)
                        nc.vector.tensor_reduce(acc[:, k % 2, s, :],
                                                adab[:, k % 2, s, DIRECT:, :].rearrange("p t d -> p d t"),
                                                AX.X, ALU.add).then_inc(acc_made, 1)
                if k >= 1:
                    dve.wait_ge(a_hi, k)
                    nc.vector.tensor_tensor(act[:, 1, k - 1, :], u32, act[:, 0, k - 1, :].bitcast(F32),
                                            ALU.subtract).then_inc(a_lo, 1)
                if k < NK:
                    dve.wait_ge(mod_done, k + 1)
                    nc.vector.tensor_tensor(mod[:, k, :], ps[:, 5, 0:2], bias_mod[:, k, :], ALU.add).then_inc(mod_made, 1)
                    dve.wait_ge(mod_made, k + 1)
                    dve.wait_ge(x_turned, k + 1)
                    for h in range(2):
                        ins = nc.vector.tensor_scalar(u32[:, h * HS:(h + 1) * HS], ps[:, 4 + h, :], mod[:, k, 0:1],
                                                      mod[:, k, 1:2], ALU.mult, ALU.add)
                    ins.then_inc(u_made, 1)
                if k % 2 == 1:
                    lo_pair(0, k + 1)
                    lo_pair(0, k + 2)
            lo_pair(0, 2 * NPAIR + 2)
            for b in range(4):
                dve.wait_ge(gemm_done, b + 1)
                nc.vector.tensor_copy(stage0[:, b], ps[:, b, :]).then_inc(dve_read, 1)
            for b in range(2):
                dve.wait_ge(gemm_done, 5 + b)
                nc.vector.tensor_copy(stage[:, b], ps[:, 6 + b, :]).then_inc(dve_read, 1)
            group(G_V)
            for b in range(2):
                dve.wait_ge(gemm_done, 7 + b)
                nc.vector.tensor_copy(stage[:, 2 + b], ps[:, 4 + b, :]).then_inc(dve_read, 1)

            def copy_banks(g):
                for b in range(4):
                    dve.wait_ge(gemm_done, g * 4 + (1 + b))
                    dve.wait_ge(stored[b], g * 16)
                    nc.vector.tensor_copy(stage[:, b], ps[:, b, :]).then_inc(dve_read, 1)

            with dve.Fori(0, 4) as i:
                group(i + G_PIN)
                copy_banks(i + G_PIN)

            with dve.Fori(0, 8) as i:
                def gate_sum(m):
                    dve.wait_ge(gmult, 2 * i + (m + 1))
                    nc.vector.tensor_reduce(acc[:, m, 0, :], adag[:, m].rearrange("p t d -> p d t"),
                                            AX.X, ALU.add).then_inc(acc_made, 1)

                def gate_col(m):
                    dve.wait_ge(gmod_done, 2 * i + (m + 1))
                    nc.vector.tensor_tensor(gcol[:, bass.ds(2 * i + m, 1)], ps[:, 6, m:m + 1],
                                            bias_gate[:, bass.ds(2 * i + m, 1)], ALU.add).then_inc(gcol_made, 1)
                group(i + G_SILU, {3: lambda: gate_sum(0), 6: lambda: (gate_col(0), gate_sum(1))})
                for b in range(4):
                    dve.wait_ge(tanh_made, i * 4 + (b + 1))
                    dve.wait_ge(stored[b], (i + G_SILU) * 16)
                    nc.vector.scalar_tensor_tensor(stage[:, b], tanhb[:, b], 1.0, ps[:, b, :], ALU.add, ALU.mult
                                                   ).then_inc(dve_read, 1)
                gate_col(1)
            dve.wait_ge(gcol_made, 16)
            nc.vector.tensor_scalar(gcol[:], gcol[:], 0.5, None, ALU.mult).then_inc(gcol_made, 1)
            nc.vector.memset(praw[:, :, 0:PAD], 0.0)
            dve.wait_ge(grow_t, 1)
            nc.vector.tensor_copy(rows[0:16, 0, :], ps[0:16, 7, 0:P]).then_inc(grow_c, 1)

            for g, w in enumerate(POOL_WINDOWS):
                def wg_split():
                    dve.wait_ge(wg_hi, g + 1)
                    nc.vector.tensor_tensor(wg[:, 1], wgraw, wg[:, 0].bitcast(F32), ALU.subtract).then_inc(wg_lo, 1)

                def pool_window(kc):
                    dve.wait_ge(p_landed, 16 * (g + 1))
                    wait(dve, pooled_lo, 2 * g + kc)
                    src, width, n = praw[:, kc], 1, g
                    while width < w:
                        dst = win[1] if n % 2 == 0 else win[0]
                        lo = 2 * width - 1
                        link(nc.vector.tensor_tensor(dst[:, lo:], src[:, lo:], src[:, lo - width:PB - width], ALU.add))
                        src, width, n = dst, 2 * width, n - 1
                    link(nc.vector.tensor_tensor(src[:, PAD:2 * PAD], src[:, PAD:2 * PAD], corr[:, g], ALU.mult))
                    nc.vector.scalar_tensor_tensor(win[1][:, PAD:], src[:, PAD:], 1.0 / w, praw[:, kc, PAD:],
                                                   ALU.mult, ALU.subtract).then_inc(win_made, 1)

                def pooled_split(kc):
                    dve.wait_ge(pooled_hi, 2 * g + kc + 1)
                    nc.vector.tensor_tensor(pooled[:, 1, kc], win[1][:, PAD:], pooled[:, 0, kc].bitcast(F32),
                                            ALU.subtract).then_inc(pooled_lo, 1)

                def mixed():
                    dve.wait_ge(ps_landed, 16 * (g + 1))
                    for b in range(4):
                        dve.wait_ge(mix_done, 4 * g + b + 1)
                        nc.vector.scalar_tensor_tensor(psilu[:, b], ps[:, 4 + b, :],
                                                       pscale[:, 2 * g + b // 2:2 * g + b // 2 + 1], psilu[:, b],
                                                       ALU.mult, ALU.mult).then_inc(mix_read, 1)
                group(g + G_Q, {0: wg_split, 1: lambda: pool_window(0),
                                3: lambda: (pooled_split(0), pool_window(1)),
                                5: lambda: pooled_split(1), 7: mixed})
                copy_banks(g + G_Q)

            nc.vector.memset(vz[:].bitcast(F32), 0.0).then_inc(vz_zeroed, 1)

            def merge_group(n, p, it, extra={}):
                first = isinstance(n, int) and n == 0
                hfs = slice(1, 2) if first else slice(0, 2)
                keys = slice(BLK, 2 * BLK) if first else slice(0, 2 * BLK)

                def tidx(par, hf):
                    return 2 * it + par if first else 4 * it - 4 + (2 * par + hf)

                def qkv_split():
                    dve.wait_ge(qkv_hi, it + 1)
                    nc.vector.tensor_tensor(qs[:, 1], qraw.rearrange("p g n -> p (g n)"), qs[:, 0].bitcast(F32),
                                            ALU.subtract)
                    nc.vector.tensor_tensor(ks[:, 1, keys], kraw[:, keys], ks[:, 0, keys].bitcast(F32), ALU.subtract)
                    for par in range(2):
                        cs = slice(par * HD, (par + 1) * HD)
                        ins = nc.vector.tensor_tensor(vz[:, 1, par, hfs, cs], vraw[:, hfs, cs],
                                                      vz[:, 0, par, hfs, cs].bitcast(F32), ALU.subtract)
                    ins.then_inc(qkv_lo, 1)

                def maxima(par):
                    dve.wait_ge(qk_done, 2 * it + par + 1)
                    dve.sem_inc(dve_steps, 1)
                    for g in range(QG):
                        off = (g % 2) * 2 * BLK
                        hd = (2 * p + par) * QG + g
                        ins = nc.vector.tensor_tensor_reduce(
                            out=prob[:, par, g, keys], in0=ps[:, 4 + g // 2, off + keys.start:off + keys.stop],
                            in1=mask[:, keys], scale=HD ** -0.5, scalar=sink[:, hd:hd + 1], op0=ALU.add,
                            op1=ALU.max, accum_out=small[:, 4 * par, g:g + 1])
                    ins.then_inc(max_made, 1)
                    dve.wait_ge(max_made, 2 * it + par + 1)
                    nc.vector.tensor_scalar(small[:, 4 * par + 1], small[:, 4 * par], -1.0, None, ALU.mult
                                            ).then_inc(neg_made, 1)
                    h0 = (2 * p + par) * QG
                    nc.vector.tensor_tensor(small[:, 4 * par + 3], sink[:, h0:h0 + QG], small[:, 4 * par],
                                            ALU.subtract).then_inc(dsink_made, 1)

                def normalise(par):
                    dve.wait_ge(exp_made, 2 * it + par + 1)
                    nc.vector.tensor_tensor(small[:, 4 * par + 2], small[:, 4 * par + 2], small[:, 4 * par + 3],
                                            ALU.add).then_inc(den_made, 1)
                    dve.wait_ge(den_made, 2 * it + par + 1)
                    nc.vector.reciprocal(small[:, 4 * par + 2], small[:, 4 * par + 2]).then_inc(rden_made, 1)
                    dve.wait_ge(rden_made, 2 * it + par + 1)
                    for g in range(QG):
                        ins = nc.vector.tensor_scalar(prob[:, par, g, keys], prob[:, par, g, keys],
                                                      small[:, 4 * par + 2, g:g + 1], None, ALU.mult)
                    ins.then_inc(prob_made, 1)

                def pt_split(par, hf):
                    if first and hf == 0:
                        return
                    dve.wait_ge(pt_hi, tidx(par, hf) + 1)
                    nc.vector.tensor_tensor(pt[:, hf, 1], ps[:, 6, :], pt[:, hf, 0].bitcast(F32), ALU.subtract
                                            ).then_inc(pt_lo, 1)

                def step(i):
                    return lambda: [f() for f in {
                        0: [qkv_split], 2: [lambda: maxima(0)], 3: [lambda: maxima(1), lambda: normalise(0)],
                        4: [lambda: pt_split(0, 0), lambda: normalise(1)], 5: [lambda: pt_split(0, 1)],
                        6: [lambda: pt_split(1, 0)], 7: [lambda: pt_split(1, 1)]}.get(i, []) + extra.get(i, [])]
                group(it + G_MERGE, {i: step(i) for i in range(NPAIR)})
                dve.wait_ge(pv_done, 2 * it + 2 if first else 4 * it)
                dve.wait_ge(asilu_landed, it * 32 + 32)
                wait(dve, yatt_stored, it * 32)
                nc.vector.scalar_tensor_tensor(yst.rearrange("p g n -> p (g n)"), ps[:, 7, :], 0.5,
                                               asilu.rearrange("p g n -> p (g n)"), ALU.mult, ALU.mult
                                               ).then_inc(yatt_made, 1)

            merge_group(0, 0, 0)
            merge_group(0, 1, 1)
            with dve.Fori(1, NB - 1) as n:
                merge_group(n, 0, 2 * n)
                merge_group(n, 1, 2 * n + 1)

            def fill_lo(f, raw):
                dve.wait_ge(a_hi, f + 1)
                nc.vector.tensor_tensor(act[:, 1, f % NK], raw[:, f % 2], act[:, 0, f % NK].bitcast(F32),
                                        ALU.subtract).then_inc(a_lo, 1)

            def y_fill(f):
                return lambda: fill_lo(f, yraw)

            def m_fill(f):
                return lambda: fill_lo(f, mraw)

            def gated(i, which):
                dve.wait_ge(tg_landed[which], i * 16 + 16)
                for b in range(4):
                    t, h = b // 2, b % 2
                    cs = slice(h * HS, (h + 1) * HS)
                    dve.wait_ge(gemm_done, i * 8 + (READ_UP + 64 + 4 * which + b + 1))
                    nc.vector.scalar_tensor_tensor(tgate[which][:, t, cs], tgate[which][:, t, cs], 1.0,
                                                   ps[:, 4 * which + b, :], ALU.add, ALU.mult).then_inc(dve_read, 1)

            def up_group(i, hooks):
                inner = hooks.get(4)
                group(i + G_UP, hooks | {4: lambda: (gated(i, 0), inner and inner())})
                gated(i, 1)
                dve.wait_ge(dve_read, i * 8 + (READ_UP + 8))
                for b in range(4):
                    t, h = b // 2, b % 2
                    cs = slice(h * HS, (h + 1) * HS)
                    nc.vector.tensor_tensor(tgate[1][:, t, cs], tgate[1][:, t, cs], tgate[0][:, t, cs], ALU.add
                                            ).then_inc(m_made, 1)

            merge_group(NB - 1, 0, 2 * NB - 2)
            merge_group(NB - 1, 1, 2 * NB - 1,
                        {i: [y_fill(NK + 2 * i - 8), y_fill(NK + 2 * i - 7)] for i in range(4, 8)})
            up_group(0, {i: (lambda i=i: (y_fill(NK + 8 + 2 * i)(), y_fill(NK + 9 + 2 * i)())) for i in range(4)})
            with dve.Fori(1, 7) as i:
                up_group(i, {})
            up_group(7, {i: (lambda i=i: (m_fill(2 * NK + 2 * i - 8)(), m_fill(2 * NK + 2 * i - 7)()))
                         for i in range(4, 8)})

            def residual(og, tiles, last_tile=False):
                h, c = og // 4, og % 4
                cols = slice(c * OC, (c + 1) * OC)
                bank = 4 * (og % 2)
                dve.wait_ge(x_in_z[c], 16 * (h + 1))
                for t in tiles:
                    dve.wait_ge(gemm_done, READ_UP + 128 + 4 * og + t + 1)
                    nc.vector.tensor_tensor(ps[:, bank + t, :], ps[:, bank + t, :], gateb[:, cols], ALU.mult
                                            ).then_inc(zg_made, 1)
                for t in tiles:
                    dve.wait_ge(zg_made, 4 * og + t + 1)
                    nc.vector.scalar_tensor_tensor(z[:, t, cols], z[:, t, cols], ALPHA, ps[:, bank + t, :],
                                                   ALU.mult, ALU.add).then_inc(dve_read, 1)
                for t in tiles:
                    dve.wait_ge(dve_read, READ_UP + 64 + 4 * og + t + 1)
                    ins = nc.vector.bn_stats(stats[:, t, c, :], z[:, t, cols])
                link(ins)

            def norm_columns(n, tiles):
                for t in tiles:
                    ins = nc.vector.bn_aggr(mv[:, t], stats[:, t].rearrange("p a s -> p (a s)"))
                link(ins)
                nc.vector.tensor_scalar(lnc[:, 0], mv[:, :, 1], EPS, None, ALU.add).then_inc(var_made, 1)
                dve.wait_ge(std_made, n + 1)
                link(nc.vector.reciprocal(lnc[:, 2], lnc[:, 1]))
                link(nc.vector.tensor_tensor(lnc[:, 3], lnc[:, 2], lnc[:, 2], ALU.mult))
                link(nc.vector.tensor_tensor(lnc[:, 3], lnc[:, 3], lnc[:, 0], ALU.mult))
                link(nc.vector.tensor_scalar(lnc[:, 3], lnc[:, 3], -0.5, 1.5, ALU.mult, ALU.add))
                link(nc.vector.tensor_tensor(lnc[:, 4], lnc[:, 2], lnc[:, 3], ALU.mult))

            def scaled(t, cols, g):
                return nc.vector.scalar_tensor_tensor(z[:, t, cols], z[:, t, cols], mv[:, t, 0:1], g,
                                                      ALU.subtract, ALU.mult)

            def shifted(t, cols, b):
                nc.vector.scalar_tensor_tensor(z[:, t, cols], z[:, t, cols], lnc[:, 4, t:t + 1], b,
                                               ALU.mult, ALU.add).then_inc(zb_made, 1)

            def norm_scale(cc):
                def go():
                    dve.wait_ge(lngb_landed[cc % 2], 32 * (cc // 2 + 1))
                    for t in range(4):
                        ins = scaled(t, slice(cc * OC, (cc + 1) * OC), lngb[:, cc % 2, 0])
                    ins.then_inc(zg2_made, 1)
                return go

            def norm_shift(cc):
                def go():
                    dve.wait_ge(zg2_made, cc + 1)
                    for t in range(4):
                        shifted(t, slice(cc * OC, (cc + 1) * OC), lngb[:, cc % 2, 1])
                return go

            def late(k):
                def go():
                    dve.wait_ge(late_hi, k + 1)
                    nc.vector.tensor_tensor(act[:, 1, k, 0:HS], lateraw[:, k % 2], act[:, 0, k, 0:HS].bitcast(F32),
                                            ALU.subtract).then_inc(late_lo, 1)
                return go

            dve.wait_ge(gateb_landed, 16)
            out_group(0, {i: m_fill(2 * NK + 8 + i) for i in range(8)})
            residual(0, range(4))
            for og in range(1, 4):
                out_group(og)
                residual(og, range(4))
            out_group(4, {1: lambda: norm_columns(0, range(4))} | {2 + 3 * cc: norm_scale(cc) for cc in range(4)}
                      | {3 + 3 * cc: norm_shift(cc) for cc in range(4)})
            residual(4, range(4))
            out_group(5, {k: late(k) for k in range(NK)})
            residual(5, range(4))
            out_group(6, last=True)
            residual(6, range(4))
            dve.wait_ge(gb_all_landed, 32)
            for t in range(4):
                residual(7, [t])
                norm_columns(1 + t, range(4))
                for cc in range(4):
                    cols = slice(cc * OC, (cc + 1) * OC)
                    scaled(t, cols, g_all[:, cols]).then_inc(zg2_made, 1)
                for cc in range(4):
                    cols = slice(cc * OC, (cc + 1) * OC)
                    dve.wait_ge(zg2_made, 4 + 4 * t + cc + 1)
                    shifted(t, cols, b_all[:, cols])


_INS = ["x", "c", "w_ada", "b_ada", "w_in", "w_pool_grp", "pool_scale", "sinks", "w_pool_up", "w_attn_up",
        "w_out", "ln_g", "ln_b"]
_OUT = ((1, S, D), "float32")


def kernel(**inputs):
    import numpy as _np
    import concourse.bacc as _bacc
    from concourse import mybir as _mybir
    from concourse.bass_utils import run_bass_kernel_spmd as _run

    nc = _bacc.Bacc("TRN2", target_bir_lowering=False, num_devices=1)
    arrays, args = {}, []
    for name in _INS:
        a = _np.ascontiguousarray(inputs[name])
        arrays[f"in_{name}_dram"] = a
        args.append(nc.dram_tensor(f"in_{name}_dram", a.shape, _mybir.dt.from_np(a.dtype), kind="ExternalInput").ap())
    args.append(nc.dram_tensor("out_0_dram", _OUT[0], _mybir.dt.from_np(_np.dtype(_OUT[1])), kind="ExternalOutput").ap())
    hybrid_layer(nc, *args)
    r = _run(nc, [arrays], core_ids=[0])
    return r.results[0]["out_0_dram"]
```

```python
from contextlib import ExitStack

import concourse.bass as bass
from concourse import mybir

F32 = mybir.dt.float32
F32R = mybir.dt.float32r
ALU = mybir.AluOpType
ACT = mybir.ActivationFunctionType
AX = mybir.AxisListType

P = 128
D = 2048
S = 1024
NK = D // P
POOL_WINDOWS = (2, 4, 8, 16)
PAD = 16
PW = 1024
AW = 1024
KVW = 256
HD = 64
BLK = 128
NB = S // BLK
QG = 4
OFF_PGATE = PW
OFF_Q = 2 * PW
OFF_K = OFF_Q + AW
OFF_V = OFF_K + KVW
OFF_AGATE = OFF_V + KVW
OFF_MERGE = OFF_AGATE + AW
ALPHA = 2.0 ** 0.25
EPS = 1e-5
MASKED = -1e30

GC = 256
HS = S // 2
NPAIR = 8
RING = 4
G_V, G_PIN, G_SILU, G_Q, G_MERGE, G_UP, G_OUT = 1, 2, 6, 14, 18, 34, 42
READ_UP = 4 * G_MERGE
OC = 512
NOUT = 8
LN_SLOT = (1, 2, 0, 1)
DIRECT = 4
REST_AT = 1
LAG = 2
PASSES = ((0, 0), (0, 1), (1, 0))


def first_pair(g):
    return NPAIR * g + NPAIR


def first_out(og):
    return first_pair(G_OUT) + NK * og


def hybrid_layer(nc, x, c, w_ada, b_ada, w_in, w_pool_grp, pool_scale, sinks,
                 w_pool_up, w_attn_up, w_out, ln_g, ln_b, out):
    with ExitStack() as ctx:
        def sb(name, shape, dt=F32):
            return ctx.enter_context(nc.sbuf_tensor(name, shape, dt))

        def sem(name):
            return ctx.enter_context(nc.semaphore(name))

        def scratch(name, shape):
            return nc.dram_tensor(name, shape, F32, kind="Internal").ap()

        d_k = scratch("d_k", (KVW, S))
        d_v = scratch("d_v", (S, KVW))
        d_p = scratch("d_p", (PW, S))
        d_silu = scratch("d_silu", (PW + AW, S))
        d_q = scratch("d_q", (AW, S))
        d_tanh = scratch("d_tanh", (2 * D, S))
        d_y = scratch("d_y", (PW + AW, S))
        d_m = scratch("d_m", (D, S))
        d_gate = scratch("d_gate", (NK, P))

        with nc.sbuf_tensor("act_raw", [P, 2, NK, S], F32) as act_raw:
            pass
        act = sb("act", [P, 2, NK, S], F32R)
        wraw = sb("wraw", [P, RING, 2, GC])
        wsp = sb("wsp", [P, RING, 2, 2, GC], F32R)
        ident = sb("ident", [P, P])
        ones = sb("ones", [P, 1])
        mask = sb("mask", [P, 2 * BLK])
        csb = sb("csb", [P, 16])
        ctanh = sb("ctanh", [P, 16])
        bias_mod = sb("bias_mod", [P, NK, 2])
        bias_gate = sb("bias_gate", [P, NK])
        mod = sb("mod", [P, NK, 2])
        gcol = sb("gcol", [P, NK])
        pscale = sb("pscale", [P, 8])
        sink = sb("sink", [P, 16])
        corr = sb("corr", [P, 4, 16])
        small = sb("small", [P, 8, 4])
        stats = sb("stats", [P, 4, 4, 6])
        mv = sb("mv", [P, 4, 2])
        lnc = sb("lnc", [P, 8, 4])
        W1 = sb("W1", [P, 8256])
        with nc.sbuf_tensor("R2", [P, 5120], F32) as R2:
            pass
        with nc.sbuf_tensor("pooled", [P, 2, 2, S], F32R) as pooled, \
                nc.sbuf_tensor("wg", [P, 2, 2, 256], F32R) as wg:
            pass
        with nc.sbuf_tensor("qs", [P, 2, QG * BLK], F32R) as qs, \
                nc.sbuf_tensor("ks", [P, 2, 2 * BLK], F32R) as ks, \
                nc.sbuf_tensor("vz", [P, 2, 2, 2, P], F32R) as vz, \
                nc.sbuf_tensor("pt", [P, 2, 2, QG * BLK], F32R) as pt:
            pass

        ada_slots = [W1[:, 4096 * n:4096 * n + 4096].rearrange("p (s t d) -> p s t d", s=2, t=16) for n in range(2)] \
            + [act_raw[:, n, 12:16, :].rearrange("p k n -> p (k n)")
               .rearrange("p (s t d) -> p s t d", s=2, t=16) for n in range(2)]
        xb = R2[:, 0:2048].rearrange("p (b t d) -> p b t d", b=2, t=8)
        u32 = R2[:, 2048:3072]
        acc = R2[:, 3072:3584].rearrange("p (b s d) -> p b s d", b=2, s=2)
        rows = R2[:, 3584:3968].rearrange("p (a d) -> p a d", a=3)
        stage = W1[:, 0:2048].rearrange("p (b n) -> p b n", b=4)
        stage0 = R2[:, 3072:5120].rearrange("p (b n) -> p b n", b=4)
        tanhb = W1[:, 2048:4096].rearrange("p (b n) -> p b n", b=4)
        adag = W1[:, 4096:8192].rearrange("p (b t d) -> p b t d", b=2, t=16)
        PB = PAD + S
        praw = W1[:, 2048:2048 + 2 * PB].rearrange("p (c n) -> p c n", c=2)
        win = [W1[:, 2048 + (2 + n) * PB:2048 + (3 + n) * PB] for n in range(2)]
        psilu = W1[:, 2048 + 4 * PB:].rearrange("p (b n) -> p b n", b=4)
        wgraw = psilu[:, 0, :].rearrange("p (c n) -> p c n", c=2)
        qraw = W1[:, 2048:2560].rearrange("p (g n) -> p g n", g=QG)
        kraw = W1[:, 2560:2816]
        vraw = W1[:, 2816:3072].rearrange("p (h n) -> p h n", h=2)
        asilu = W1[:, 3072:3584].rearrange("p (g n) -> p g n", g=QG)
        yst = W1[:, 3584:4096].rearrange("p (g n) -> p g n", g=QG)
        prob = W1[:, 4096:6144].rearrange("p (h g n) -> p h g n", h=2, g=QG)
        tgate = [W1[:, 2048 * n:2048 * n + 2048].rearrange("p (t n) -> p t n", t=2) for n in range(2)]
        fill_raw = [W1[:, 6144 + n * S:6144 + (n + 1) * S] for n in range(2)] \
            + [R2[:, 1024 + n * S:1024 + (n + 1) * S] for n in range(4)]
        z = W1[:, 0:8192].rearrange("p (t n) -> p t n", t=4)
        gateb = R2[:, 0:2048]
        lateraw = R2[:, 2048:3072].rearrange("p (b n) -> p b n", b=2)
        g_all = R2[:, 3072:5120]
        b_all = wraw.rearrange("p s k n -> p (s k n)")
        lngb = R2[:, 2048:5120].rearrange("p (b s n) -> p b s n", b=3, s=2)

        ps = ctx.enter_context(nc.psum_tensor("ps", [P, 8, 512], F32))

        pool_steps = sem("pool_steps")
        dve_steps = sem("dve_steps")
        setup_in = sem("setup_in")
        consts = sem("consts")
        ones_made = sem("ones_made")
        cols_t = sem("cols_t")
        cols_c = sem("cols_c")
        c_tanh = sem("c_tanh")
        w_landed = [sem(f"w_landed{n}") for n in range(RING)]
        w_hi = sem("w_hi")
        w_lo = sem("w_lo")
        w_used = sem("w_used")
        x_landed = [sem(f"x_landed{n}") for n in range(2)]
        ada_landed = [[sem(f"ada_landed{n}_{s}") for s in range(2)] for n in range(4)]
        x_turned = sem("x_turned")
        ada_mult = sem("ada_mult")
        acc_made = sem("acc_made")
        mod_done = sem("mod_done")
        mod_made = sem("mod_made")
        u_made = sem("u_made")
        a_hi = sem("a_hi")
        a_lo = sem("a_lo")
        gemm_done = sem("gemm_done")
        dve_read = sem("dve_read")
        act_read = sem("act_read")
        tanh_made = sem("tanh_made")
        stored = [sem(f"stored{n}") for n in range(4)]
        agate_landed = [sem(f"agate_landed{n}") for n in range(2)]
        gmult = sem("gmult")
        gmod_done = sem("gmod_done")
        gcol_made = sem("gcol_made")
        grow_t = sem("grow_t")
        grow_c = sem("grow_c")
        grow_stored = sem("grow_stored")
        p_landed = sem("p_landed")
        wg_landed = sem("wg_landed")
        ps_landed = sem("ps_landed")
        chain = sem("chain")
        win_made = sem("win_made")
        pooled_hi = sem("pooled_hi")
        pooled_lo = sem("pooled_lo")
        wg_hi = sem("wg_hi")
        wg_lo = sem("wg_lo")
        mix_done = sem("mix_done")
        mix_read = sem("mix_read")
        ypool_stored = sem("ypool_stored")
        vz_zeroed = sem("vz_zeroed")
        q_landed = sem("q_landed")
        asilu_landed = sem("asilu_landed")
        qkv_hi = sem("qkv_hi")
        qkv_lo = sem("qkv_lo")
        qk_done = sem("qk_done")
        max_made = sem("max_made")
        neg_made = sem("neg_made")
        dsink_made = sem("dsink_made")
        exp_made = sem("exp_made")
        den_made = sem("den_made")
        rden_made = sem("rden_made")
        prob_made = sem("prob_made")
        turned = sem("turned")
        pt_hi = sem("pt_hi")
        pt_lo = sem("pt_lo")
        pv_done = sem("pv_done")
        yatt_made = sem("yatt_made")
        yatt_stored = sem("yatt_stored")
        tg_landed = [sem(f"tg_landed{n}") for n in range(2)]
        m_made = sem("m_made")
        m_stored = sem("m_stored")
        fill_landed = [sem(f"fill_landed{n}") for n in range(6)]
        gateb_landed = sem("gateb_landed")
        x_in_z = [sem(f"x_in_z{n}") for n in range(4)]
        late_landed = [sem(f"late_landed{n}") for n in range(2)]
        late_hi = sem("late_hi")
        late_lo = sem("late_lo")
        gb_all_landed = sem("gb_all_landed")
        zg_made = sem("zg_made")
        var_made = sem("var_made")
        std_made = sem("std_made")
        lngb_landed = [sem(f"lngb_landed{n}") for n in range(3)]
        zg2_made = sem("zg2_made")
        zb_made = sem("zb_made")
        out_stored = [sem(f"out_stored{n}") for n in range(4)]
        tail_stored = sem("tail_stored")

        def wait(eng, s, value):
            if not isinstance(value, int) or value > 0:
                eng.wait_ge(s, value)

        ada_v = w_ada[0].rearrange("(t p) n -> p t n", p=P)
        x_v = x[0].rearrange("(t p) d -> p t d", p=P)
        out_v = out[0].rearrange("(t p) d -> p t d", p=P)
        w_v = [w.rearrange("(k p) n -> p k n", p=P) for w in (w_in[0], w_pool_up[0], w_attn_up[0], w_out[0])]
        IN, PUP, AUP, OUT = range(4)

        ada_slot = [k % 4 if k < 12 else k % 2 for k in range(NK)]

        def uses(slots, k):
            return sum(slots[m] == slots[k] for m in range(k + 1))

        def before(slots, k):
            return max((m for m in range(k) if slots[m] == slots[k]), default=None)

        fill_slot = [None] * NK + [2 + f % 4 if 10 <= f - NK < 14 or f >= 2 * NK else f % 2 for f in range(NK, 3 * NK)]

        block = ctx.enter_context(nc.Block())

        @block.sync
        def _(sp):
            def load(q, slot, dst, src):
                wait(sp, w_lo, q - RING + 1)
                sp.dma_start(dst, src).then_inc(w_landed[slot], 16)

            def load_pair(g, j, which, col, k0):
                load(first_pair(g) + j, j % RING, wraw[:, j % RING], w_v[which][:, k0:k0 + 2, bass.ds(col, GC)])

            sp.dma_start(rows[0:16, 0, :], c[0].rearrange("(t p) -> t p", p=P)).then_inc(setup_in, 16)
            sp.dma_start(rows[0:48, 1, :], b_ada[0].rearrange("(t p) -> t p", p=P)).then_inc(setup_in, 16)
            sp.dma_start(rows[0:8, 2, :], pool_scale[0].rearrange("(t p) -> t p", p=P)).then_inc(setup_in, 16)
            sp.dma_start(sink[:], sinks[0].partition_broadcast(P)).then_inc(setup_in, 16)
            def load_ada(k):
                prev = before(ada_slot, k)
                for s, off in ((0, D), (1, 0)):
                    if prev is not None:
                        sp.wait_ge(mod_done, 2 * prev + s + 1)
                    sp.dma_start(ada_slots[ada_slot[k]][:, s], ada_v[:, :, off + k * P:off + (k + 1) * P]).then_inc(
                        ada_landed[ada_slot[k]][s], 16)

            load_ada(0)
            for k in range(NK):
                wait(sp, x_turned, k - 1)
                sp.dma_start(xb[:, k % 2], x_v[:, :, k * P:(k + 1) * P]).then_inc(x_landed[k % 2], 16)
                if k + 1 < NK:
                    load_ada(k + 1)
                if k % 2 == 0:
                    for n, off in ((k, OFF_K), (k + 1, OFF_V)):
                        load(n, n % RING, wraw[:, n % RING], w_v[IN][:, k:k + 2, off:off + GC])
            for j in range(NPAIR):
                load_pair(G_V, j, IN, OFF_V, 2 * j)
            with sp.Fori(0, 4) as i:
                for j in range(NPAIR):
                    load_pair(i + G_PIN, j, IN, i * GC, 2 * j)
            sp.wait_ge(mod_done, 2 * NK)
            for part, off in ((0, OFF_PGATE), (1, OFF_AGATE)):
                with sp.Fori(0, 4) as i:
                    for j in range(NPAIR):
                        load_pair(i + (G_SILU + 4 * part), j, IN, i * GC + off, 2 * j)
                        if j % 4 == 1:
                            m = j // 4
                            sp.wait_ge(acc_made, 2 * i + (2 * NK + 8 * part + m - 1))
                            sp.dma_start(adag[:, m], ada_v[:, :, bass.ds(i * GC + (2 * D + (8 * part + m) * P), P)]
                                         ).then_inc(agate_landed[m], 16)
            with sp.Fori(0, 4) as i:
                for j in range(NPAIR):
                    load_pair(i + G_Q, j, IN, i * GC + OFF_Q, 2 * j)
            with sp.Fori(0, 16) as i:
                for j in range(NPAIR):
                    load_pair(i + G_MERGE, j, IN, i * GC + OFF_MERGE, 2 * j)
            with sp.Fori(0, 8) as i:
                for j in range(NPAIR):
                    load_pair(i + G_UP, j, PUP if j < 4 else AUP, i * GC, 2 * (j % 4))

            def load_out(og, k, c):
                load(first_out(og) + k, k % RING, wraw[:, k % RING].rearrange("p k n -> p (k n)"),
                     w_out[0][k * P:(k + 1) * P, bass.ds(c * OC, OC)])

            with sp.Fori(0, 4) as i:
                for k in range(NK):
                    load_out(i, k, i)
            for chunk in range(3):
                for k in range(NK):
                    load_out(4 + chunk, k, chunk)
                    m = (chunk - 1) * NK + k - 3
                    if 0 <= m < NK:
                        if m == 0:
                            sp.wait_ge(zb_made, 12)
                        wait(sp, late_lo, m - 1)
                        sp.dma_start(lateraw[:, m % 2], w_out[0][m * P:(m + 1) * P, 3 * OC:]).then_inc(
                            late_landed[m % 2], 16)
            for cc in range(4):
                sp.wait_ge(out_stored[cc], 16)
            sp.wait_ge(tail_stored, 16 * (2 * 3 + 4))

        @block.gpsimd
        def _(pool):
            def start(dst, src):
                pool.sem_inc(pool_steps, 1)
                return pool.dma_start(dst, src)

            nc.gpsimd.memset(ident[:], 0.0).then_inc(consts, 1)
            nc.gpsimd.memset(mask[:], 0.0).then_inc(consts, 1)
            pool.wait_ge(consts, 2)
            nc.gpsimd.affine_select(out=ident[:], in_=ident[:], compare_op=ALU.not_equal, fill=1.0, base=0,
                                    pattern=[[-1, P]], channel_multiplier=1).then_inc(consts, 1)
            nc.gpsimd.affine_select(out=mask[:, 0:BLK], in_=mask[:, 0:BLK], compare_op=ALU.is_gt, fill=MASKED,
                                    base=0, pattern=[[1, BLK]], channel_multiplier=-1).then_inc(consts, 1)
            nc.gpsimd.affine_select(out=mask[:, BLK:], in_=mask[:, BLK:], compare_op=ALU.is_ge, fill=MASKED,
                                    base=0, pattern=[[-1, BLK]], channel_multiplier=1).then_inc(consts, 1)
            for t in range(16):
                nc.gpsimd.memset(corr[:, :, t], float(t + 1)).then_inc(consts, 1)

            def store_banks(dst, row, ready, count, src=stage):
                for b in range(4):
                    t, h = b // 2, b % 2
                    pool.wait_ge(ready, count + b + 1)
                    start(dst[bass.ds(row + t * P, P), h * HS:(h + 1) * HS], src[:, b]).then_inc(stored[b], 16)

            store_banks(d_k, 0, dve_read, 0, stage0)
            for b in range(4):
                pool.wait_ge(dve_read, 4 + b + 1)
                start(d_v[2 * b * P:(2 * b + 2) * P, :].rearrange("(t p) n -> p t n", p=P),
                               stage[:, b].rearrange("p (t n) -> p t n", t=2)).then_inc(stored[b], 16)
            with pool.Fori(0, 4) as i:
                store_banks(d_p, i * GC, dve_read, (i + G_PIN) * 4)
            with pool.Fori(0, 8) as i:
                store_banks(d_silu, i * GC, dve_read, (i + G_SILU) * 4)
            pool.wait_ge(grow_c, 1)
            start(d_gate[:, :], rows[0:16, 0, :]).then_inc(grow_stored, 16)

            def mixer_io(i, middle=None):
                pool.wait_ge(dve_read, (i + G_Q) * 4)
                for b in range(4):
                    pool.wait_ge(stored[b], 16 * G_Q)
                start(praw[:, :, PAD:], d_p[bass.ds(i * GC, GC), :].rearrange("(c p) n -> p c n", p=P)
                      ).then_inc(p_landed, 16)
                start(wgraw, w_pool_grp[0].rearrange("g r n -> (g r) n")[bass.ds(i * GC, GC), :]
                      .rearrange("(c p) n -> p c n", p=P)).then_inc(wg_landed, 16)
                pool.wait_ge(wg_lo, i + 1)
                start(psilu.rearrange("p (t h) n -> p t (h n)", t=2),
                      d_silu[bass.ds(i * GC, GC), :].rearrange("(t p) n -> p t n", p=P)).then_inc(ps_landed, 16)
                if middle is not None:
                    middle()
                for b in range(4):
                    t, h = b // 2, b % 2
                    pool.wait_ge(mix_read, i * 4 + (b + 1))
                    start(d_y[bass.ds(i * GC + t * P, P), h * HS:(h + 1) * HS], psilu[:, b]).then_inc(ypool_stored, 16)

            with pool.Fori(0, 3) as i:
                mixer_io(i)
                store_banks(d_q, i * GC, dve_read, (i + G_Q) * 4)
                pool.wait_ge(ypool_stored, i * 64 + 64)

            def load_qkv(n, p, it):
                wait(pool, qkv_lo, it)
                first = isinstance(n, int) and n == 0
                for par in range(2):
                    src = d_q[(2 * p + par) * QG * HD:(2 * p + par + 1) * QG * HD, bass.ds(n * BLK, BLK)]
                    start(qraw[par * HD:(par + 1) * HD], src.rearrange("(g d) n -> d g n", d=HD)
                                   ).then_inc(q_landed, 16)
                if first:
                    start(kraw[:, BLK:], d_k[p * P:(p + 1) * P, 0:BLK]).then_inc(q_landed, 16)
                    start(vraw[:, 1], d_v[0:BLK, p * P:(p + 1) * P]).then_inc(q_landed, 16)
                else:
                    start(kraw, d_k[p * P:(p + 1) * P, bass.ds((n - 1) * BLK, 2 * BLK)]
                                   ).then_inc(q_landed, 16)
                    start(vraw, d_v[bass.ds((n - 1) * BLK, 2 * BLK), p * P:(p + 1) * P]
                                   .rearrange("(h k) n -> k h n", h=2)).then_inc(q_landed, 16)

            def load_asilu(n, p, it):
                wait(pool, yatt_made, it)
                for par in range(2):
                    r = PW + (2 * p + par) * QG * HD
                    start(asilu[par * HD:(par + 1) * HD],
                                   d_silu[r:r + QG * HD, bass.ds(n * BLK, BLK)].rearrange("(g d) n -> d g n", d=HD)
                                   ).then_inc(asilu_landed, 16)

            def store_yatt(n, p, it):
                pool.wait_ge(yatt_made, it + 1)
                for par in range(2):
                    r = PW + (2 * p + par) * QG * HD
                    start(d_y[r:r + QG * HD, bass.ds(n * BLK, BLK)].rearrange("(g d) n -> d g n", d=HD),
                                   yst[par * HD:(par + 1) * HD]).then_inc(yatt_stored, 16)

            def first_operands():
                pool.wait_ge(win_made, 8)
                load_qkv(0, 0, 0)
                load_asilu(0, 0, 0)
            mixer_io(3, first_operands)
            store_banks(d_q, 3 * GC, dve_read, (3 + G_Q) * 4)
            for b in range(4):
                pool.wait_ge(stored[b], 16 * G_MERGE)

            def merge_group(n, p, it, after):
                if after is not None:
                    load_qkv(*after)
                store_yatt(n, p, it)
                if after is not None:
                    load_asilu(*after)
                store_banks(d_tanh, it * GC, act_read, it * 4)

            merge_group(0, 0, 0, (0, 1, 1))
            merge_group(0, 1, 1, (1, 0, 2))
            with pool.Fori(1, NB - 1) as n:
                merge_group(n, 0, 2 * n, (n, 1, 2 * n + 1))
                merge_group(n, 1, 2 * n + 1, (n + 1, 0, 2 * n + 2))
            merge_group(NB - 1, 0, 2 * NB - 2, (NB - 1, 1, 2 * NB - 1))

            def load_fill(f):
                prev, slot = before(fill_slot, f), fill_slot[f]
                if prev is not None:
                    pool.wait_ge(a_lo, prev + 1)
                start(fill_raw[slot], (d_y if f < 2 * NK else d_m)[(f % NK) * P:(f % NK + 1) * P, :]
                      ).then_inc(fill_landed[slot], 16)

            pool.wait_ge(ypool_stored, 16 * 16)
            for f in range(NK, NK + 8):
                load_fill(f)
            merge_group(NB - 1, 1, 2 * NB - 1, None)
            for b in range(4):
                pool.wait_ge(stored[b], 16 * G_UP)
            pool.wait_ge(yatt_stored, 16 * 2 * 2 * NB)
            for f in range(NK + 8, NK + 14):
                load_fill(f)
            for which in range(2):
                start(tgate[which], d_tanh[which * D:which * D + GC, :].rearrange("(t p) n -> p t n", p=P)
                      ).then_inc(tg_landed[which], 16)
            for f in range(NK + 14, 2 * NK):
                load_fill(f)

            def up_stores(i, load_next):
                for t in range(2):
                    pool.wait_ge(m_made, i * 4 + 2 * t + 2)
                    start(d_m[bass.ds(i * GC + t * P, P), :], tgate[1][:, t]).then_inc(m_stored, 16)
                if load_next:
                    start(tgate[0], d_tanh[bass.ds(i * GC + GC, GC), :].rearrange("(t p) n -> p t n", p=P)
                                   ).then_inc(tg_landed[0], 16)
                    pool.wait_ge(m_stored, i * 32 + 32)
                    start(tgate[1], d_tanh[bass.ds(i * GC + (D + GC), GC), :]
                                   .rearrange("(t p) n -> p t n", p=P)).then_inc(tg_landed[1], 16)

            with pool.Fori(0, 7) as i:
                up_stores(i, True)

            def store_out(cc):
                pool.wait_ge(zb_made, (cc + 1) * 4)
                cols = slice(cc * OC, (cc + 1) * OC)
                start(out_v[:, 0:4, cols], z[:, :, cols]).then_inc(out_stored[cc], 16)
                pool.wait_ge(out_stored[cc], 16)
                start(z[:, :, cols], x_v[:, 4:8, cols]).then_inc(x_in_z[cc], 16)

            pool.wait_ge(m_stored, 7 * 32)
            for f in range(2 * NK, 2 * NK + 12):
                load_fill(f)
            up_stores(7, False)
            pool.wait_ge(m_stored, 8 * 32)
            for f in range(2 * NK + 12, 3 * NK):
                load_fill(f)
            for c in range(4):
                start(z[:, :, c * OC:(c + 1) * OC], x_v[:, 0:4, c * OC:(c + 1) * OC]).then_inc(x_in_z[c], 16)
            pool.wait_ge(a_lo, 3 * NK)
            pool.wait_ge(grow_stored, 16)
            start(gateb, d_gate.rearrange("t p -> (t p)").partition_broadcast(P)).then_inc(gateb_landed, 16)

            for cc in range(4):
                wait(pool, zb_made, (cc - 2) * 4)
                for s, src in ((0, ln_g), (1, ln_b)):
                    start(lngb[:, LN_SLOT[cc], s], src[0, cc * OC:(cc + 1) * OC].partition_broadcast(P)
                          ).then_inc(lngb_landed[LN_SLOT[cc]], 16)
                if cc == 2:
                    store_out(0)
            for cc in range(1, 4):
                store_out(cc)
            start(g_all, ln_g[0].partition_broadcast(P)).then_inc(gb_all_landed, 16)
            pool.wait_ge(w_lo, first_out(NOUT - 1))
            start(b_all, ln_b[0].partition_broadcast(P)).then_inc(gb_all_landed, 16)
            for t in range(4):
                parts = 4 if t == 3 else 2
                for n in range(parts):
                    w = D // parts
                    pool.wait_ge(zb_made, 16 + 4 * t + (n + 1) * 4 // parts)
                    start(out_v[:, 4 + t, n * w:(n + 1) * w], z[:, t, n * w:(n + 1) * w]).then_inc(tail_stored, 16)

        @block.tensor
        def _(pe):
            def product(dst, stat, mov, first, last, done=None, start=None, between=None):
                for n, (a, b) in enumerate(PASSES):
                    mm = nc.tensor.matmul(dst, stat(a), mov(b), start=first and n == 0, stop=last and n == 2)
                    if n == 0 and start is not None:
                        mm.then_inc(start, 1)
                    if n == 2 and done is not None:
                        mm.then_inc(done, 1)
                    if between is not None:
                        between(n)

            def begin_pair(g, j):
                pe.wait_ge(w_lo, first_pair(g) + (j + 1))

            def group_rows(g, reuse, nk=NK, j0=0, kt0=0, bank0=0, hooks=None, fill0=None):
                for k in range(nk):
                    j = j0 + k // 2
                    if k % 2 == 0:
                        begin_pair(g, j)
                    if hooks and k in hooks:
                        hooks[k]()
                    if fill0 is not None:
                        pe.wait_ge(a_lo, fill0 + kt0 + k + 1)
                    for b in range(4):
                        t, h = b // 2, b % 2
                        if k == 0:
                            reuse(b)
                        product(ps[:, bank0 + b, :],
                                lambda a: wsp[:, j % RING, a, k % 2, t * P:(t + 1) * P],
                                lambda a: act[:, a, kt0 + k, h * HS:(h + 1) * HS],
                                k == 0, k == nk - 1,
                                done=gemm_done if k == nk - 1 else None,
                                start=w_used if k % 2 == 0 and b == 0 else None)

            pe.wait_ge(consts, 5)
            pe.wait_ge(setup_in, 64)
            nc.tensor.transpose(ps[:, 7, 0:16], rows[0:16, 0, :], ident[0:16, 0:16])
            nc.tensor.transpose(ps[:, 7, 64:112], rows[0:48, 1, :], ident[0:48, 0:48])
            nc.tensor.transpose(ps[:, 7, 128:136], rows[0:8, 2, :], ident[0:8, 0:8]).then_inc(cols_t, 1)

            def turn_x(k, h):
                for t in range(4):
                    mm = nc.tensor.transpose(ps[:, 4 + h, t * P:(t + 1) * P], xb[:, k % 2, 4 * h + t, :], ident[:])
                return mm

            def v_step(k, t0, bank0, slot, used, after={}):
                for t in range(4):
                    for n, (a, b) in enumerate(PASSES):
                        mm = nc.tensor.matmul(ps[:, bank0 + t // 2, (t % 2) * GC:(t % 2 + 1) * GC],
                                              act[:, a, k, (t0 + t) * P:(t0 + t + 1) * P],
                                              wsp[:, slot, b, k % 2, :], start=k == 0 and n == 0 and t % 2 == 0,
                                              stop=k == NK - 1 and n == 2, skip_group_check=True)
                        if n == 0 and t == 0 and used:
                            mm.then_inc(w_used, 1)
                    if k == NK - 1 and t % 2 == 1:
                        mm.then_inc(gemm_done, 1)
                    if t in after:
                        after[t]()

            for k in range(NK + LAG):
                def direct(n):
                    s, t = n // DIRECT, n % DIRECT
                    if t == 0:
                        pe.wait_ge(ada_landed[ada_slot[k]][s], 16 * uses(ada_slot, k))
                    nc.tensor.matmul(ps[:, 5, s:s + 1], ada_slots[ada_slot[k]][:, s, t, :], csb[:, t:t + 1],
                                     start=s == 0 and t == 0, stop=False, skip_group_check=True)

                def mod_columns():
                    for s in range(2):
                        pe.wait_ge(acc_made, 2 * k + s + 1)
                        if k == 0:
                            pe.wait_ge(ones_made, 1)
                        nc.tensor.matmul(ps[:, 5, s:s + 1], acc[:, k % 2, s, :], ones[:], start=False, stop=True,
                                         skip_group_check=True).then_inc(mod_done, 1)

                def turn_rest():
                    pe.wait_ge(mod_made, k + 1)
                    turn_x(k, 1).then_inc(x_turned, 1)

                def turn_first():
                    pe.wait_ge(x_landed[k % 2], 16 * (k // 2 + 1))
                    wait(pe, u_made, k)
                    turn_x(k, 0)

                if k == 0:
                    pe.wait_ge(cols_c, 6)
                if k >= LAG:
                    kt = k - LAG
                    j = kt // 2
                    if kt % 2 == 0:
                        pe.wait_ge(w_lo, 2 * j + 1)
                    pe.wait_ge(a_lo, kt + 1)
                    for b in range(4):
                        t, h = b // 2, b % 2

                        def between(n):
                            m = (b - 1) * len(PASSES) + n
                            if k < NK and 0 <= m < 2 * DIRECT:
                                direct(m)
                        product(ps[:, b, :],
                                lambda a: wsp[:, 2 * j % RING, a, kt % 2, t * P:(t + 1) * P],
                                lambda a: act[:, a, kt, h * HS:(h + 1) * HS],
                                kt == 0, kt == NK - 1, done=gemm_done if kt == NK - 1 else None,
                                start=w_used if kt and kt % 2 == 0 and b == 0 else None, between=between)
                        if k < NK and b == 0:
                            turn_first()
                    if kt % 2 == 0:
                        pe.wait_ge(w_lo, 2 * j + 2)
                    v_step(kt, 0, 6, (2 * j + 1) % RING, kt % 2 == 1,
                           {0: mod_columns, REST_AT: turn_rest} if k < NK else {})
                else:
                    turn_first()
                    for n in range(2 * DIRECT):
                        direct(n)
                    mod_columns()
                    turn_rest()

            for k in range(NK):
                if k % 2 == 0:
                    begin_pair(G_V, k // 2)
                v_step(k, 4, 4, (k // 2) % RING, k % 2 == 0)

            def after_dve(g):
                return lambda b: pe.wait_ge(dve_read, g * 4 + (b - 3))

            with pe.Fori(0, 4) as i:
                group_rows(i + G_PIN, after_dve(i + G_PIN))

            with pe.Fori(0, 8) as i:
                def gate_chunk(m):
                    def go():
                        pe.wait_ge(acc_made, 2 * i + (2 * NK + m + 1))
                        nc.tensor.matmul(ps[:, 6, m:m + 1], acc[:, m, 0, :], ones[:], start=True, stop=True
                                         ).then_inc(gmod_done, 1)
                    return go
                group_rows(i + G_SILU, after_dve(i + G_SILU), hooks={9: gate_chunk(0)})
                gate_chunk(1)()
            pe.wait_ge(gcol_made, 17)
            nc.tensor.transpose(ps[0:16, 7, 0:P], gcol[:], ident[:]).then_inc(grow_t, 1)

            with pe.Fori(0, 4) as i:
                def mixer():
                    pe.wait_ge(wg_lo, i + 1)
                    pe.wait_ge(pooled_lo, 2 * i + 2)
                    for b in range(4):
                        t, h = b // 2, b % 2
                        for kc in range(2):
                            product(ps[:, 4 + b, :],
                                    lambda a: wg[:, a, kc, t * P:(t + 1) * P],
                                    lambda a: pooled[:, a, kc, h * HS:(h + 1) * HS],
                                    kc == 0, kc == 1, done=mix_done if kc else None)
                group_rows(i + G_Q, after_dve(i + G_Q), hooks={12: mixer})

            def merge_group(n, p, it, reuse):
                first = isinstance(n, int) and n == 0
                halves = (1,) if first else (0, 1)
                keys = slice(BLK, 2 * BLK) if first else slice(0, 2 * BLK)

                def tidx(par, hf):
                    return 2 * it + par if first else 4 * it - 4 + (2 * par + hf)

                def scores(par):
                    def go():
                        if par == 0:
                            pe.wait_ge(qkv_lo, it + 1)
                        wait(pe, max_made, 2 * it + par)
                        rows_ = slice(par * HD, (par + 1) * HD)
                        for g in range(QG):
                            off = (g % 2) * 2 * BLK
                            product(ps[:, 4 + g // 2, off + keys.start:off + keys.stop],
                                    lambda a: qs[rows_, a, g * BLK:(g + 1) * BLK],
                                    lambda a: ks[rows_, a, keys], True, True,
                                    done=qk_done if g == QG - 1 else None)
                    return go

                def turn(par, hf):
                    def go():
                        pe.wait_ge(prob_made, 2 * it + par + 1)
                        wait(pe, pt_lo, tidx(par, hf))
                        for g in range(QG):
                            mm = nc.tensor.transpose(ps[:, 6, g * BLK:(g + 1) * BLK],
                                                     prob[:, par, g, hf * BLK:(hf + 1) * BLK], ident[:])
                        mm.then_inc(turned, 1)
                    return go

                def pv(par):
                    def go():
                        if par == 0:
                            wait(pe, yatt_made, it)
                        for hf in halves:
                            pe.wait_ge(pt_lo, tidx(par, hf) + 1)
                            product(ps[:, 7, :], lambda a: vz[:, a, par, hf, :], lambda a: pt[:, hf, a, :],
                                    par == 0 and hf == halves[0], par == 1 and hf == 1, done=pv_done)
                    return go

                def both(*f):
                    return lambda: [g() for g in f]
                hooks = {2: scores(0), 5: scores(1), 10: turn(0, 1), 14: turn(1, 1)}
                if first:
                    hooks |= {12: pv(0)}
                else:
                    hooks |= {8: turn(0, 0), 12: both(turn(1, 0), pv(0))}
                group_rows(it + G_MERGE, reuse, hooks=hooks)
                pv(1)()

            def after_act(it):
                return lambda b: pe.wait_ge(act_read, it * 4 + (b - 3))

            pe.wait_ge(mix_read, 16)
            merge_group(0, 0, 0, after_dve(G_MERGE))
            merge_group(0, 1, 1, after_act(1))
            with pe.Fori(1, NB) as n:
                merge_group(n, 0, 2 * n, after_act(2 * n))
                merge_group(n, 1, 2 * n + 1, after_act(2 * n + 1))

            def up_group(i, reuse_a, reuse_b, fill):
                group_rows(i + G_UP, reuse_a, nk=8, fill0=fill)
                group_rows(i + G_UP, reuse_b, nk=8, j0=4, kt0=8, bank0=4, fill0=fill)

            up_group(0, lambda b: pe.wait_ge(act_read, 61 + b), lambda b: pe.wait_ge(yatt_made, 2 * NB), NK)
            with pe.Fori(1, 8) as i:
                up_group(i, lambda b: pe.wait_ge(dve_read, i * 8 + (READ_UP - 8 + b + 1)),
                         lambda b: pe.wait_ge(dve_read, i * 8 + (READ_UP - 4 + b + 1)), None)

            def out_group(og, h, st):
                for k in range(NK):
                    pe.wait_ge(w_lo, first_out(og) + (k + 1))
                    if h == 0:
                        pe.wait_ge(a_lo, 2 * NK + k + 1)
                    for t in range(4):
                        if k == 0:
                            pe.wait_ge(dve_read, og * 4 + (READ_UP + 57 + t))
                        product(ps[:, 4 * st + t, :],
                                lambda a: act[:, a, k, h * HS + t * P:h * HS + (t + 1) * P],
                                lambda a: wsp[:, k % RING, a].rearrange("p k n -> p (k n)"),
                                k == 0, k == NK - 1, done=gemm_done if k == NK - 1 else None,
                                start=w_used if t == 0 else None)

            with pe.Fori(0, 2) as i:
                out_group(2 * i, 0, 0)
                out_group(2 * i + 1, 0, 1)
            for c in range(3):
                out_group(4 + c, 1, c % 2)
            for t in range(4):
                pe.wait_ge(dve_read, (NOUT - 1) * 4 + (READ_UP + 57 + t))
                for k in range(NK):
                    if t == 0:
                        pe.wait_ge(late_lo, k + 1)
                    product(ps[:, 4 + t, :],
                            lambda a: act[:, a, k, HS + t * P:HS + (t + 1) * P],
                            lambda a: act[:, a, k, 0:HS],
                            k == 0, k == NK - 1, done=gemm_done if k == NK - 1 else None)

        @block.scalar
        def _(act_e):
            def hi_pair(q0, i):
                s = i % RING
                act_e.wait_ge(w_landed[s], q0 * (16 // RING) + 16 * (i // RING + 1))
                wait(act_e, w_used, q0 + (i - RING + 1))
                nc.scalar.copy(wsp[:, s, 0].rearrange("p k n -> p (k n)"),
                               wraw[:, s].rearrange("p k n -> p (k n)")).then_inc(w_hi, 1)

            def group(g, hooks=None):
                for i in range(NPAIR):
                    hi_pair(first_pair(g), i + 3)
                    if hooks and i in hooks:
                        hooks[i]()

            def out_group(og, hooks=None, last=False):
                for i in range(NK):
                    if not last or i + 3 < NK:
                        hi_pair(first_out(og), i + 3)
                    if hooks and i in hooks:
                        hooks[i]()

            act_e.wait_ge(cols_t, 1)
            nc.scalar.activation(ctanh[:], ps[:, 7, 0:16], ACT.Tanh, scale=0.5).then_inc(c_tanh, 1)
            act_e.wait_ge(cols_c, 6)
            for k in range(NK + 1):
                def ada_products(s):
                    if k < NK:
                        act_e.wait_ge(ada_landed[ada_slot[k]][s], 16 * uses(ada_slot, k))
                        for t in range(DIRECT, 16):
                            w = ada_slots[ada_slot[k]][:, s, t, :]
                            ins = nc.scalar.activation(w, w, ACT.Identity, scale=csb[:, t:t + 1])
                        ins.then_inc(ada_mult, 1)
                for s in range(2):
                    ada_products(s)
                if k >= 1:
                    act_e.wait_ge(u_made, k)
                    nc.scalar.copy(act[:, 0, k - 1, :], u32).then_inc(a_hi, 1)
                if k % 2 == 1:
                    hi_pair(0, k - 1)
                    hi_pair(0, k)
            for i in range(3):
                hi_pair(0, 2 * NPAIR + i)
            group(G_V)
            with act_e.Fori(0, 4) as i:
                group(i + G_PIN)

            with act_e.Fori(0, 8) as i:
                def gate_mult(m):
                    def go():
                        act_e.wait_ge(agate_landed[m], i * 16 + 16)
                        for t in range(16):
                            ins = nc.scalar.activation(adag[:, m, t, :], adag[:, m, t, :], ACT.Identity,
                                                       scale=csb[:, t:t + 1])
                        ins.then_inc(gmult, 1)
                    return go
                group(i + G_SILU, {2: gate_mult(0), 5: gate_mult(1)})
                for b in range(4):
                    act_e.wait_ge(gemm_done, (i + G_SILU) * 4 + (1 + b))
                    act_e.wait_ge(dve_read, (i + G_SILU) * 4 + (b - 3))
                    nc.scalar.activation(tanhb[:, b], ps[:, b, :], ACT.Tanh, scale=0.5).then_inc(tanh_made, 1)

            with act_e.Fori(0, 4) as i:
                def split_wg():
                    act_e.wait_ge(wg_landed, i * 16 + 16)
                    nc.scalar.copy(wg[:, 0].rearrange("p c n -> p (c n)"),
                                   wgraw.rearrange("p c n -> p (c n)")).then_inc(wg_hi, 1)

                def split_pooled(kc):
                    def go():
                        act_e.wait_ge(win_made, 2 * i + (kc + 1))
                        nc.scalar.copy(pooled[:, 0, kc, :], win[1][:, PAD:]).then_inc(pooled_hi, 1)
                    return go
                group(i + G_Q, {0: split_wg, 2: split_pooled(0), 4: split_pooled(1)})

            def merge_group(n, p, it, extra={}):
                first = isinstance(n, int) and n == 0
                hfs = slice(1, 2) if first else slice(0, 2)
                keys = slice(BLK, 2 * BLK) if first else slice(0, 2 * BLK)

                def tidx(par, hf):
                    return 2 * it + par if first else 4 * it - 4 + (2 * par + hf)

                def split_qkv():
                    act_e.wait_ge(q_landed, it * 64 + 64)
                    if not first or it:
                        act_e.wait_ge(pv_done, 2 * it if first else 4 * it - 4)
                    nc.scalar.copy(qs[:, 0], qraw.rearrange("p g n -> p (g n)"))
                    nc.scalar.copy(ks[:, 0, keys], kraw[:, keys])
                    for par in range(2):
                        cs = slice(par * HD, (par + 1) * HD)
                        ins = nc.scalar.copy(vz[:, 0, par, hfs, cs], vraw[:, hfs, cs])
                    ins.then_inc(qkv_hi, 1)

                def exps(par):
                    act_e.wait_ge(neg_made, 2 * it + par + 1)
                    for g in range(QG):
                        nc.scalar.activation(prob[:, par, g, keys], prob[:, par, g, keys], ACT.Exp,
                                             bias=small[:, 4 * par + 1, g:g + 1],
                                             accum_out=small[:, 4 * par + 2, g:g + 1])
                    act_e.wait_ge(dsink_made, 2 * it + par + 1)
                    nc.scalar.activation(small[:, 4 * par + 3], small[:, 4 * par + 3], ACT.Exp).then_inc(exp_made, 1)

                def pt_split(par, hf):
                    if first and hf == 0:
                        return
                    act_e.wait_ge(turned, tidx(par, hf) + 1)
                    if first:
                        wait(act_e, pv_done, tidx(par, hf))
                    else:
                        wait(act_e, pv_done, tidx(par, hf) - 1)
                    nc.scalar.copy(pt[:, hf, 0], ps[:, 6, :]).then_inc(pt_hi, 1)

                def step(i):
                    return lambda: [f() for f in {
                        0: [split_qkv], 2: [lambda: exps(0)], 3: [lambda: exps(1)],
                        4: [lambda: pt_split(0, 0)], 5: [lambda: pt_split(0, 1)],
                        6: [lambda: pt_split(1, 0)], 7: [lambda: pt_split(1, 1)]}.get(i, []) + extra.get(i, [])]
                group(it + G_MERGE, {i: step(i) for i in range(NPAIR)})
                for b in range(4):
                    act_e.wait_ge(gemm_done, it * 4 + (4 * G_MERGE + 1 + b))
                    act_e.wait_ge(stored[b], it * 16 + 16 * G_MERGE)
                    nc.scalar.activation(stage[:, b], ps[:, b, :], ACT.Tanh, scale=0.5).then_inc(act_read, 1)

            act_e.wait_ge(vz_zeroed, 1)
            merge_group(0, 0, 0)
            merge_group(0, 1, 1)
            with act_e.Fori(1, NB - 1) as n:
                merge_group(n, 0, 2 * n)
                merge_group(n, 1, 2 * n + 1)

            def fill_hi(f, last_user):
                slot = fill_slot[f]
                act_e.wait_ge(fill_landed[slot], 16 * uses(fill_slot, f))
                act_e.wait_ge(w_used, first_pair(last_user) + (f % NK) // 2 + 1)
                nc.scalar.copy(act[:, 0, f % NK, :], fill_raw[slot]).then_inc(a_hi, 1)

            def y_fill(f):
                return lambda: fill_hi(f, G_UP - 1)

            def m_fill(f):
                return lambda: fill_hi(f, G_OUT - 1)

            merge_group(NB - 1, 0, 2 * NB - 2)
            merge_group(NB - 1, 1, 2 * NB - 1,
                        {i: [y_fill(NK + 2 * i - 8), y_fill(NK + 2 * i - 7)] for i in range(4, 8)})
            group(G_UP, {i: (lambda i=i: (y_fill(NK + 8 + 2 * i)(), y_fill(NK + 9 + 2 * i)())) for i in range(4)})
            with act_e.Fori(1, 7) as i:
                group(i + G_UP)
            group(G_OUT - 1, {i: (lambda i=i: (m_fill(2 * NK + 2 * i - 8)(), m_fill(2 * NK + 2 * i - 7)()))
                              for i in range(4, 8)})

            def square_root(n):
                act_e.wait_ge(var_made, n + 1)
                nc.scalar.activation(lnc[:, 1], lnc[:, 0], ACT.Sqrt).then_inc(std_made, 1)

            def late(k):
                def go():
                    act_e.wait_ge(late_landed[k % 2], 16 * (k // 2 + 1))
                    if k == 0:
                        act_e.wait_ge(w_used, first_out(4))
                    nc.scalar.copy(act[:, 0, k, 0:HS], lateraw[:, k % 2]).then_inc(late_hi, 1)
                return go

            out_group(0, {i: m_fill(2 * NK + 8 + i) for i in range(8)})
            for og in range(1, 4):
                out_group(og)
            out_group(4, {1: lambda: square_root(0)})
            out_group(5, {k: late(k) for k in range(NK)})
            out_group(6, last=True)
            for t in range(4):
                square_root(1 + t)

        @block.vector
        def _(dve):
            links = [0]

            def link(ins):
                links[0] += 1
                ins.then_inc(chain, 1)
                dve.wait_ge(chain, links[0])

            def lo_pair(q0, i):
                s = i % RING
                dve.wait_ge(w_hi, q0 + (i + 1))
                nc.vector.tensor_tensor(wsp[:, s, 1], wraw[:, s], wsp[:, s, 0].bitcast(F32),
                                        ALU.subtract).then_inc(w_lo, 1)

            def group(g, hooks=None):
                for i in range(NPAIR):
                    lo_pair(first_pair(g), i + 3)
                    if hooks and i in hooks:
                        hooks[i]()

            def out_group(og, hooks=None, last=False):
                for i in range(NK):
                    if not last or i + 3 < NK:
                        lo_pair(first_out(og), i + 3)
                    if hooks and i in hooks:
                        hooks[i]()

            nc.vector.memset(ones[:], 1.0).then_inc(ones_made, 1)
            dve.wait_ge(c_tanh, 1)
            nc.vector.scalar_tensor_tensor(csb[:], ctanh[:], 1.0, ps[:, 7, 0:16], ALU.add, ALU.mult).then_inc(cols_c, 1)
            dve.wait_ge(cols_c, 1)
            nc.vector.tensor_scalar(csb[:], csb[:], 0.5, None, ALU.mult).then_inc(cols_c, 1)
            nc.vector.tensor_scalar(bias_mod[:, :, 0], ps[:, 7, 80:96], 1.0, None, ALU.add).then_inc(cols_c, 1)
            nc.vector.tensor_copy(bias_mod[:, :, 1], ps[:, 7, 64:80]).then_inc(cols_c, 1)
            nc.vector.tensor_copy(bias_gate[:], ps[:, 7, 96:112]).then_inc(cols_c, 1)
            nc.vector.tensor_scalar(pscale[:], ps[:, 7, 128:136], 0.5, None, ALU.mult).then_inc(cols_c, 1)
            dve.wait_ge(cols_c, 6)
            dve.wait_ge(consts, 21)
            link(nc.vector.reciprocal(corr[:], corr[:]))
            for g, w in enumerate(POOL_WINDOWS):
                nc.vector.tensor_scalar(corr[:, g], corr[:, g], float(w), 1.0, ALU.mult, ALU.max)

            for k in range(NK + 1):
                def ada_sum(s):
                    if k < NK:
                        dve.wait_ge(ada_mult, 2 * k + s + 1)
                        nc.vector.tensor_reduce(acc[:, k % 2, s, :],
                                                ada_slots[ada_slot[k]][:, s, DIRECT:, :].rearrange("p t d -> p d t"),
                                                AX.X, ALU.add).then_inc(acc_made, 1)
                for s in range(2):
                    ada_sum(s)
                if k >= 1:
                    dve.wait_ge(a_hi, k)
                    nc.vector.tensor_tensor(act[:, 1, k - 1, :], u32, act[:, 0, k - 1, :].bitcast(F32),
                                            ALU.subtract).then_inc(a_lo, 1)
                if k < NK:
                    dve.wait_ge(mod_done, 2 * k + 2)
                    nc.vector.tensor_tensor(mod[:, k, :], ps[:, 5, 0:2], bias_mod[:, k, :], ALU.add).then_inc(mod_made, 1)
                    dve.wait_ge(mod_made, k + 1)
                    dve.wait_ge(x_turned, k + 1)
                    for h in range(2):
                        ins = nc.vector.tensor_scalar(u32[:, h * HS:(h + 1) * HS], ps[:, 4 + h, :], mod[:, k, 0:1],
                                                      mod[:, k, 1:2], ALU.mult, ALU.add)
                    ins.then_inc(u_made, 1)
                if k % 2 == 1:
                    lo_pair(0, k - 1)
                    lo_pair(0, k)
            for i in range(3):
                lo_pair(0, 2 * NPAIR + i)
            for b in range(4):
                dve.wait_ge(gemm_done, b + 1)
                nc.vector.tensor_copy(stage0[:, b], ps[:, b, :]).then_inc(dve_read, 1)
            for b in range(2):
                dve.wait_ge(gemm_done, 5 + b)
                nc.vector.tensor_copy(stage[:, b], ps[:, 6 + b, :]).then_inc(dve_read, 1)
            group(G_V)
            for b in range(2):
                dve.wait_ge(gemm_done, 7 + b)
                nc.vector.tensor_copy(stage[:, 2 + b], ps[:, 4 + b, :]).then_inc(dve_read, 1)

            def copy_banks(g):
                for b in range(4):
                    dve.wait_ge(gemm_done, g * 4 + (1 + b))
                    dve.wait_ge(stored[b], g * 16)
                    nc.vector.tensor_copy(stage[:, b], ps[:, b, :]).then_inc(dve_read, 1)

            with dve.Fori(0, 4) as i:
                group(i + G_PIN)
                copy_banks(i + G_PIN)

            with dve.Fori(0, 8) as i:
                def gate_sum(m):
                    dve.wait_ge(gmult, 2 * i + (m + 1))
                    nc.vector.tensor_reduce(acc[:, m, 0, :], adag[:, m].rearrange("p t d -> p d t"),
                                            AX.X, ALU.add).then_inc(acc_made, 1)

                def gate_col(m):
                    dve.wait_ge(gmod_done, 2 * i + (m + 1))
                    nc.vector.tensor_tensor(gcol[:, bass.ds(2 * i + m, 1)], ps[:, 6, m:m + 1],
                                            bias_gate[:, bass.ds(2 * i + m, 1)], ALU.add).then_inc(gcol_made, 1)
                group(i + G_SILU, {3: lambda: gate_sum(0), 6: lambda: (gate_col(0), gate_sum(1))})
                for b in range(4):
                    dve.wait_ge(tanh_made, i * 4 + (b + 1))
                    dve.wait_ge(stored[b], (i + G_SILU) * 16)
                    nc.vector.scalar_tensor_tensor(stage[:, b], tanhb[:, b], 1.0, ps[:, b, :], ALU.add, ALU.mult
                                                   ).then_inc(dve_read, 1)
                gate_col(1)
            dve.wait_ge(gcol_made, 16)
            nc.vector.tensor_scalar(gcol[:], gcol[:], 0.5, None, ALU.mult).then_inc(gcol_made, 1)
            nc.vector.memset(praw[:, :, 0:PAD], 0.0)
            dve.wait_ge(grow_t, 1)
            nc.vector.tensor_copy(rows[0:16, 0, :], ps[0:16, 7, 0:P]).then_inc(grow_c, 1)

            for g, w in enumerate(POOL_WINDOWS):
                def wg_split():
                    dve.wait_ge(wg_hi, g + 1)
                    nc.vector.tensor_tensor(wg[:, 1], wgraw, wg[:, 0].bitcast(F32), ALU.subtract).then_inc(wg_lo, 1)

                def pool_window(kc):
                    dve.wait_ge(p_landed, 16 * (g + 1))
                    wait(dve, pooled_lo, 2 * g + kc)
                    src, width, n = praw[:, kc], 1, g
                    while width < w:
                        dst = win[1] if n % 2 == 0 else win[0]
                        lo = 2 * width - 1
                        link(nc.vector.tensor_tensor(dst[:, lo:], src[:, lo:], src[:, lo - width:PB - width], ALU.add))
                        src, width, n = dst, 2 * width, n - 1
                    link(nc.vector.tensor_tensor(src[:, PAD:2 * PAD], src[:, PAD:2 * PAD], corr[:, g], ALU.mult))
                    nc.vector.scalar_tensor_tensor(win[1][:, PAD:], src[:, PAD:], 1.0 / w, praw[:, kc, PAD:],
                                                   ALU.mult, ALU.subtract).then_inc(win_made, 1)

                def pooled_split(kc):
                    dve.wait_ge(pooled_hi, 2 * g + kc + 1)
                    nc.vector.tensor_tensor(pooled[:, 1, kc], win[1][:, PAD:], pooled[:, 0, kc].bitcast(F32),
                                            ALU.subtract).then_inc(pooled_lo, 1)

                def mixed():
                    dve.wait_ge(ps_landed, 16 * (g + 1))
                    for b in range(4):
                        dve.wait_ge(mix_done, 4 * g + b + 1)
                        nc.vector.scalar_tensor_tensor(psilu[:, b], ps[:, 4 + b, :],
                                                       pscale[:, 2 * g + b // 2:2 * g + b // 2 + 1], psilu[:, b],
                                                       ALU.mult, ALU.mult).then_inc(mix_read, 1)
                group(g + G_Q, {0: lambda: (wg_split(), pool_window(0)),
                                2: lambda: (pooled_split(0), pool_window(1)),
                                4: lambda: pooled_split(1), 7: mixed})
                copy_banks(g + G_Q)

            nc.vector.memset(vz[:].bitcast(F32), 0.0).then_inc(vz_zeroed, 1)

            def merge_group(n, p, it, extra={}):
                first = isinstance(n, int) and n == 0
                hfs = slice(1, 2) if first else slice(0, 2)
                keys = slice(BLK, 2 * BLK) if first else slice(0, 2 * BLK)

                def tidx(par, hf):
                    return 2 * it + par if first else 4 * it - 4 + (2 * par + hf)

                def qkv_split():
                    dve.wait_ge(qkv_hi, it + 1)
                    nc.vector.tensor_tensor(qs[:, 1], qraw.rearrange("p g n -> p (g n)"), qs[:, 0].bitcast(F32),
                                            ALU.subtract)
                    nc.vector.tensor_tensor(ks[:, 1, keys], kraw[:, keys], ks[:, 0, keys].bitcast(F32), ALU.subtract)
                    for par in range(2):
                        cs = slice(par * HD, (par + 1) * HD)
                        ins = nc.vector.tensor_tensor(vz[:, 1, par, hfs, cs], vraw[:, hfs, cs],
                                                      vz[:, 0, par, hfs, cs].bitcast(F32), ALU.subtract)
                    ins.then_inc(qkv_lo, 1)

                def maxima(par):
                    dve.wait_ge(qk_done, 2 * it + par + 1)
                    dve.sem_inc(dve_steps, 1)
                    for g in range(QG):
                        off = (g % 2) * 2 * BLK
                        hd = (2 * p + par) * QG + g
                        ins = nc.vector.tensor_tensor_reduce(
                            out=prob[:, par, g, keys], in0=ps[:, 4 + g // 2, off + keys.start:off + keys.stop],
                            in1=mask[:, keys], scale=HD ** -0.5, scalar=sink[:, hd:hd + 1], op0=ALU.add,
                            op1=ALU.max, accum_out=small[:, 4 * par, g:g + 1])
                    ins.then_inc(max_made, 1)
                    dve.wait_ge(max_made, 2 * it + par + 1)
                    nc.vector.tensor_scalar(small[:, 4 * par + 1], small[:, 4 * par], -1.0, None, ALU.mult
                                            ).then_inc(neg_made, 1)
                    h0 = (2 * p + par) * QG
                    nc.vector.tensor_tensor(small[:, 4 * par + 3], sink[:, h0:h0 + QG], small[:, 4 * par],
                                            ALU.subtract).then_inc(dsink_made, 1)

                def normalise(par):
                    dve.wait_ge(exp_made, 2 * it + par + 1)
                    nc.vector.tensor_tensor(small[:, 4 * par + 2], small[:, 4 * par + 2], small[:, 4 * par + 3],
                                            ALU.add).then_inc(den_made, 1)
                    dve.wait_ge(den_made, 2 * it + par + 1)
                    nc.vector.reciprocal(small[:, 4 * par + 2], small[:, 4 * par + 2]).then_inc(rden_made, 1)
                    dve.wait_ge(rden_made, 2 * it + par + 1)
                    for g in range(QG):
                        ins = nc.vector.tensor_scalar(prob[:, par, g, keys], prob[:, par, g, keys],
                                                      small[:, 4 * par + 2, g:g + 1], None, ALU.mult)
                    ins.then_inc(prob_made, 1)

                def pt_split(par, hf):
                    if first and hf == 0:
                        return
                    dve.wait_ge(pt_hi, tidx(par, hf) + 1)
                    nc.vector.tensor_tensor(pt[:, hf, 1], ps[:, 6, :], pt[:, hf, 0].bitcast(F32), ALU.subtract
                                            ).then_inc(pt_lo, 1)

                def step(i):
                    return lambda: [f() for f in {
                        0: [qkv_split], 1: [lambda: maxima(0)], 3: [lambda: maxima(1), lambda: normalise(0)],
                        4: [lambda: pt_split(0, 0), lambda: normalise(1)], 5: [lambda: pt_split(0, 1)],
                        6: [lambda: pt_split(1, 0)], 7: [lambda: pt_split(1, 1)]}.get(i, []) + extra.get(i, [])]
                group(it + G_MERGE, {i: step(i) for i in range(NPAIR)})
                dve.wait_ge(pv_done, 2 * it + 2 if first else 4 * it)
                dve.wait_ge(asilu_landed, it * 32 + 32)
                wait(dve, yatt_stored, it * 32)
                nc.vector.scalar_tensor_tensor(yst.rearrange("p g n -> p (g n)"), ps[:, 7, :], 0.5,
                                               asilu.rearrange("p g n -> p (g n)"), ALU.mult, ALU.mult
                                               ).then_inc(yatt_made, 1)

            merge_group(0, 0, 0)
            merge_group(0, 1, 1)
            with dve.Fori(1, NB - 1) as n:
                merge_group(n, 0, 2 * n)
                merge_group(n, 1, 2 * n + 1)

            def fill_lo(f):
                def go():
                    dve.wait_ge(a_hi, f + 1)
                    nc.vector.tensor_tensor(act[:, 1, f % NK], fill_raw[fill_slot[f]],
                                            act[:, 0, f % NK].bitcast(F32), ALU.subtract).then_inc(a_lo, 1)
                return go

            def gated(i, which):
                dve.wait_ge(tg_landed[which], i * 16 + 16)
                for b in range(4):
                    t, h = b // 2, b % 2
                    cs = slice(h * HS, (h + 1) * HS)
                    dve.wait_ge(gemm_done, i * 8 + (READ_UP + 64 + 4 * which + b + 1))
                    nc.vector.scalar_tensor_tensor(tgate[which][:, t, cs], tgate[which][:, t, cs], 1.0,
                                                   ps[:, 4 * which + b, :], ALU.add, ALU.mult).then_inc(dve_read, 1)

            def up_group(i, hooks):
                inner = hooks.get(4)
                group(i + G_UP, hooks | {4: lambda: (gated(i, 0), inner and inner())})
                gated(i, 1)
                dve.wait_ge(dve_read, i * 8 + (READ_UP + 8))
                for b in range(4):
                    t, h = b // 2, b % 2
                    cs = slice(h * HS, (h + 1) * HS)
                    nc.vector.tensor_tensor(tgate[1][:, t, cs], tgate[1][:, t, cs], tgate[0][:, t, cs], ALU.add
                                            ).then_inc(m_made, 1)

            merge_group(NB - 1, 0, 2 * NB - 2)
            merge_group(NB - 1, 1, 2 * NB - 1,
                        {i: [fill_lo(NK + 2 * i - 8), fill_lo(NK + 2 * i - 7)] for i in range(4, 8)})
            up_group(0, {i: (lambda i=i: (fill_lo(NK + 8 + 2 * i)(), fill_lo(NK + 9 + 2 * i)())) for i in range(4)})
            with dve.Fori(1, 7) as i:
                up_group(i, {})
            up_group(7, {i: (lambda i=i: (fill_lo(2 * NK + 2 * i - 8)(), fill_lo(2 * NK + 2 * i - 7)()))
                         for i in range(4, 8)})

            def residual(og, tiles):
                h, c = og // 4, og % 4
                cols = slice(c * OC, (c + 1) * OC)
                bank = 4 * (og % 2)
                dve.wait_ge(x_in_z[c], 16 * (h + 1))
                for t in tiles:
                    dve.wait_ge(gemm_done, READ_UP + 128 + 4 * og + t + 1)
                    nc.vector.tensor_tensor(ps[:, bank + t, :], ps[:, bank + t, :], gateb[:, cols], ALU.mult
                                            ).then_inc(zg_made, 1)
                for t in tiles:
                    dve.wait_ge(zg_made, 4 * og + t + 1)
                    nc.vector.scalar_tensor_tensor(z[:, t, cols], z[:, t, cols], ALPHA, ps[:, bank + t, :],
                                                   ALU.mult, ALU.add).then_inc(dve_read, 1)

            def statistics(og, tiles):
                c = og % 4
                for t in tiles:
                    dve.wait_ge(dve_read, READ_UP + 64 + 4 * og + t + 1)
                    ins = nc.vector.bn_stats(stats[:, t, c, :], z[:, t, c * OC:(c + 1) * OC])
                link(ins)

            def norm_columns(n, tiles):
                for t in tiles:
                    ins = nc.vector.bn_aggr(mv[:, t], stats[:, t].rearrange("p a s -> p (a s)"))
                link(ins)
                nc.vector.tensor_scalar(lnc[:, 0], mv[:, :, 1], EPS, None, ALU.add).then_inc(var_made, 1)
                dve.wait_ge(std_made, n + 1)
                link(nc.vector.reciprocal(lnc[:, 2], lnc[:, 1]))
                link(nc.vector.tensor_tensor(lnc[:, 3], lnc[:, 2], lnc[:, 2], ALU.mult))
                link(nc.vector.tensor_tensor(lnc[:, 3], lnc[:, 3], lnc[:, 0], ALU.mult))
                link(nc.vector.tensor_scalar(lnc[:, 3], lnc[:, 3], -0.5, 1.5, ALU.mult, ALU.add))
                link(nc.vector.tensor_tensor(lnc[:, 4], lnc[:, 2], lnc[:, 3], ALU.mult))

            def scaled(t, cols, g):
                return nc.vector.scalar_tensor_tensor(z[:, t, cols], z[:, t, cols], mv[:, t, 0:1], g,
                                                      ALU.subtract, ALU.mult)

            def shifted(t, cols, b):
                nc.vector.scalar_tensor_tensor(z[:, t, cols], z[:, t, cols], lnc[:, 4, t:t + 1], b,
                                               ALU.mult, ALU.add).then_inc(zb_made, 1)

            def norm_scale(cc):
                def go():
                    dve.wait_ge(lngb_landed[LN_SLOT[cc]], 32 * (cc // 3 + 1))
                    for t in range(4):
                        ins = scaled(t, slice(cc * OC, (cc + 1) * OC), lngb[:, LN_SLOT[cc], 0])
                    ins.then_inc(zg2_made, 1)
                return go

            def norm_shift(cc):
                def go():
                    dve.wait_ge(zg2_made, cc + 1)
                    for t in range(4):
                        shifted(t, slice(cc * OC, (cc + 1) * OC), lngb[:, LN_SLOT[cc], 1])
                return go

            def late(k):
                def go():
                    dve.wait_ge(late_hi, k + 1)
                    nc.vector.tensor_tensor(act[:, 1, k, 0:HS], lateraw[:, k % 2], act[:, 0, k, 0:HS].bitcast(F32),
                                            ALU.subtract).then_inc(late_lo, 1)
                return go

            out_group(0, {i: fill_lo(2 * NK + 8 + i) for i in range(8)})
            dve.wait_ge(gateb_landed, 16)
            residual(0, range(4))
            for og in range(1, 4):
                out_group(og, {0: lambda: statistics(og - 1, range(4))})
                residual(og, range(4))
            out_group(4, {0: lambda: statistics(3, range(4)), 1: lambda: norm_columns(0, range(4))}
                      | {2 + 3 * cc: norm_scale(cc) for cc in range(4)} | {3 + 3 * cc: norm_shift(cc) for cc in range(4)})
            residual(4, range(4))
            out_group(5, {k: late(k) for k in range(1, NK)} | {0: lambda: (statistics(4, range(4)), late(0)())})
            residual(5, range(4))
            out_group(6, {0: lambda: statistics(5, range(4))}, last=True)
            residual(6, range(4))
            statistics(6, range(4))
            dve.wait_ge(gb_all_landed, 32)
            for t in range(4):
                residual(7, [t])
                statistics(7, [t])
                norm_columns(1 + t, [t])
                for cc in range(4):
                    cols = slice(cc * OC, (cc + 1) * OC)
                    scaled(t, cols, g_all[:, cols]).then_inc(zg2_made, 1)
                for cc in range(4):
                    cols = slice(cc * OC, (cc + 1) * OC)
                    dve.wait_ge(zg2_made, 4 + 4 * t + cc + 1)
                    shifted(t, cols, b_all[:, cols])


_INS = ["x", "c", "w_ada", "b_ada", "w_in", "w_pool_grp", "pool_scale", "sinks", "w_pool_up", "w_attn_up",
        "w_out", "ln_g", "ln_b"]
_OUT = ((1, S, D), "float32")


def kernel(**inputs):
    import numpy as _np
    import concourse.bacc as _bacc
    from concourse import mybir as _mybir
    from concourse.bass_utils import run_bass_kernel_spmd as _run

    nc = _bacc.Bacc("TRN2", target_bir_lowering=False, num_devices=1)
    arrays, args = {}, []
    for name in _INS:
        a = _np.ascontiguousarray(inputs[name])
        arrays[f"in_{name}_dram"] = a
        args.append(nc.dram_tensor(f"in_{name}_dram", a.shape, _mybir.dt.from_np(a.dtype), kind="ExternalInput").ap())
    args.append(nc.dram_tensor("out_0_dram", _OUT[0], _mybir.dt.from_np(_np.dtype(_OUT[1])), kind="ExternalOutput").ap())
    hybrid_layer(nc, *args)
    r = _run(nc, [arrays], core_ids=[0])
    return r.results[0]["out_0_dram"]
```
